# Optimizing a Trainium2 kernel written in Bass

```python
import jax, jax.numpy as jnp
from jax import lax
import numpy as np

D_MODEL = 1024
BATCH = 1
SEQ = 512
DEPTH = 1

N_MIXERS = 2
POOL_EXPAND = 2
D_POOL = POOL_EXPAND * D_MODEL
POOL_WINDOWS = (2, 4, 8, 16)
N_POOL_GROUPS = len(POOL_WINDOWS)
POOL_GROUP = D_POOL // N_POOL_GROUPS
HEAD_DIM = 64
N_HEADS = D_MODEL // HEAD_DIM
N_KV = 4
HPG = N_HEADS // N_KV
D_ATT = N_HEADS * HEAD_DIM
D_KV = N_KV * HEAD_DIM
N_BRANCH = 3
CMP_BLOCK = 32
CMP_STRIDE = 16
CMP_HIDDEN = 4 * HEAD_DIM
SEL_BLOCK = 64
SEL_TOPN = 8
WINDOW = 256
Q_BLOCK = 64
NSA_SPLITS = (D_ATT, D_KV, D_KV, D_KV, D_KV, D_KV, D_KV, D_ATT, N_BRANCH * N_HEADS)
NSA_VALUE_SLOTS = (2, 4, 6)
D_NSA_IN = sum(NSA_SPLITS)

N_POOL_LAYERS = (DEPTH + N_MIXERS - 1) // N_MIXERS
N_NSA_LAYERS = DEPTH // N_MIXERS

DN_ALPHA = (2.0 * DEPTH) ** 0.25
DN_BETA = (8.0 * DEPTH) ** -0.25
LN_EPS = 1e-5
NEG_INF = -1e30
FORCE_SCORE = 1e9


def layer_norm(x, g, b):
    xf = x.astype(jnp.float32)
    mu = jnp.mean(xf, axis=-1, keepdims=True)
    var = jnp.mean(jnp.square(xf - mu), axis=-1, keepdims=True)
    y = (xf - mu) * lax.rsqrt(var + LN_EPS) * g.astype(jnp.float32) + b.astype(jnp.float32)
    return y.astype(x.dtype)

def alibi_slopes():
    h = jnp.arange(1, N_HEADS + 1, dtype=jnp.float32)
    return (2.0 ** (-8.0 * h / N_HEADS)).reshape(N_KV, HPG)

def masked_softmax(s, valid):
    p = jax.nn.softmax(jnp.where(valid, s, NEG_INF), axis=-1)
    return jnp.where(valid, p, 0.0)

def pool_mixer(x, w_in, w_grp, scale, w_out):
    B, S, _ = x.shape
    h = x @ w_in
    u, z = h[..., :D_POOL], h[..., D_POOL:]
    u = u.astype(jnp.float32).reshape(B, S, N_POOL_GROUPS, POOL_GROUP)
    csum = jnp.cumsum(u, axis=1)
    t = jnp.arange(S)
    outs = []
    for g, w in enumerate(POOL_WINDOWS):
        c = csum[:, :, g]
        lag = jnp.pad(c, ((0, 0), (w, 0), (0, 0)))[:, :S]
        cnt = jnp.minimum(t + 1, w).astype(jnp.float32)[None, :, None]
        outs.append((c - lag) / cnt - u[:, :, g])
    m = jnp.stack(outs, axis=2).astype(x.dtype)
    m = jnp.einsum('bsgc,gcd->bsgd', m, w_grp).reshape(B, S, D_POOL) * scale
    return (m * jax.nn.silu(z)) @ w_out

def nsa_mixer(x, w_in, pos_k, w1_k, w2_k, pos_v, w1_v, w2_v, w_out):
    B, S, _ = x.shape
    dt = x.dtype
    h = x @ w_in
    q, kc, vc, ks, vs, kw, vw, z, gl = jnp.split(h, np.cumsum(NSA_SPLITS)[:-1].tolist(), axis=-1)
    q = q.reshape(B, S, N_KV, HPG, HEAD_DIM) * (HEAD_DIM ** -0.5)
    kc, vc, ks, vs, kw, vw = [a.reshape(B, S, N_KV, HEAD_DIM) for a in (kc, vc, ks, vs, kw, vw)]
    gates = jax.nn.sigmoid(gl.astype(jnp.float32)).reshape(B, S, N_KV, HPG, N_BRANCH)
    slopes = alibi_slopes()[None, :, :, None, None]

    n_cmp = (S - CMP_BLOCK) // CMP_STRIDE + 1
    cmp_idx = np.arange(n_cmp)[:, None] * CMP_STRIDE + np.arange(CMP_BLOCK)[None, :]
    cmp_end = jnp.asarray(cmp_idx[:, -1], dtype=jnp.int32)

    def compress(a, pos, w1, w2):
        blk = a[:, cmp_idx] + pos[None, None, :, None, :]
        blk = blk.transpose(0, 1, 3, 2, 4).reshape(B, n_cmp, N_KV, CMP_BLOCK * HEAD_DIM)
        return jax.nn.silu(blk @ w1) @ w2

    k_cmp = compress(kc, pos_k, w1_k, w2_k)
    v_cmp = compress(vc, pos_v, w1_v, w2_v)

    n_sel = S // SEL_BLOCK
    top_n = min(SEL_TOPN, n_sel)
    c0 = np.arange(n_cmp)[:, None] * CMP_STRIDE
    j0 = np.arange(n_sel)[None, :] * SEL_BLOCK
    overlap = jnp.asarray((c0 < j0 + SEL_BLOCK) & (c0 + CMP_BLOCK > j0), dtype=jnp.float32)
    ks_blk = ks.reshape(B, n_sel, SEL_BLOCK, N_KV, HEAD_DIM).transpose(0, 3, 1, 2, 4)
    vs_blk = vs.reshape(B, n_sel, SEL_BLOCK, N_KV, HEAD_DIM).transpose(0, 3, 1, 2, 4)
    b_ix = jnp.arange(B)[:, None, None, None]
    g_ix = jnp.arange(N_KV)[None, :, None, None]
    blk_ids = jnp.arange(n_sel)
    in_blk = jnp.arange(SEL_BLOCK)

    kw_pad = jnp.pad(kw, ((0, 0), (WINDOW, 0), (0, 0), (0, 0)))
    vw_pad = jnp.pad(vw, ((0, 0), (WINDOW, 0), (0, 0), (0, 0)))
    win_off = jnp.arange(WINDOW + Q_BLOCK) - WINDOW

    def block(i):
        q0 = i * Q_BLOCK
        qb = lax.dynamic_slice_in_dim(q, q0, Q_BLOCK, axis=1)
        gb = lax.dynamic_slice_in_dim(gates, q0, Q_BLOCK, axis=1)
        t = q0 + jnp.arange(Q_BLOCK)

        dist = t[:, None] - cmp_end[None, :]
        s = jnp.einsum('bqghd,bcgd->bghqc', qb, k_cmp).astype(jnp.float32)
        s = s - slopes * dist.astype(jnp.float32)
        p_cmp = masked_softmax(s, dist >= 0)
        o_cmp = jnp.einsum('bghqc,bcgd->bqghd', p_cmp.astype(dt), v_cmp)

        imp = jnp.einsum('bghqc,cn->bgqn', p_cmp, overlap)
        cur = t // SEL_BLOCK
        forced = (blk_ids[None] == 0) | (blk_ids[None] == cur[:, None]) | (blk_ids[None] == cur[:, None] - 1)
        future = blk_ids[None] > cur[:, None]
        imp = jnp.where(forced, FORCE_SCORE, jnp.where(future, NEG_INF, imp))
        _, sel = lax.top_k(imp, top_n)
        k_g = ks_blk[b_ix, g_ix, sel].reshape(B, N_KV, Q_BLOCK, top_n * SEL_BLOCK, HEAD_DIM)
        v_g = vs_blk[b_ix, g_ix, sel].reshape(B, N_KV, Q_BLOCK, top_n * SEL_BLOCK, HEAD_DIM)
        pos = (sel[..., None] * SEL_BLOCK + in_blk).reshape(B, N_KV, Q_BLOCK, top_n * SEL_BLOCK)
        dist = t[None, None, :, None] - pos
        s = jnp.einsum('bqghd,bgqkd->bghqk', qb, k_g).astype(jnp.float32)
        s = s - slopes * dist[:, :, None].astype(jnp.float32)
        p = masked_softmax(s, (dist >= 0)[:, :, None])
        o_sel = jnp.einsum('bghqk,bgqkd->bqghd', p.astype(dt), v_g)

        kwb = lax.dynamic_slice_in_dim(kw_pad, q0, WINDOW + Q_BLOCK, axis=1)
        vwb = lax.dynamic_slice_in_dim(vw_pad, q0, WINDOW + Q_BLOCK, axis=1)
        spos = q0 + win_off
        dist = t[:, None] - spos[None, :]
        valid = (dist >= 0) & (dist < WINDOW) & (spos[None, :] >= 0)
        s = jnp.einsum('bqghd,bkgd->bghqk', qb, kwb).astype(jnp.float32)
        s = s - slopes * dist.astype(jnp.float32)
        p = masked_softmax(s, valid)
        o_win = jnp.einsum('bghqk,bkgd->bqghd', p.astype(dt), vwb)

        o = gb[..., 0:1] * o_cmp + gb[..., 1:2] * o_sel + gb[..., 2:3] * o_win
        return o.astype(dt).reshape(B, Q_BLOCK, D_ATT)

    o = lax.map(block, jnp.arange(S // Q_BLOCK))
    o = o.transpose(1, 0, 2, 3).reshape(B, S, D_ATT)
    return (o * jax.nn.silu(z)) @ w_out

def first_inputs(seed: int = 0) -> dict:
    key = jax.random.key(seed)
    k = jax.random.split(key, 16)
    nA, nB = N_POOL_LAYERS, N_NSA_LAYERS

    def nrm(kk, shape, scale):
        return jax.random.normal(kk, shape, jnp.float32) * scale

    pool_col = jnp.asarray(np.concatenate([np.full(D_POOL, DN_BETA), np.ones(D_POOL)]), dtype=jnp.float32)
    nsa_col = jnp.asarray(np.concatenate([np.full(n, DN_BETA if s in NSA_VALUE_SLOTS else 1.0)
                                          for s, n in enumerate(NSA_SPLITS)]), dtype=jnp.float32)
    return {
        'x': nrm(k[0], (BATCH, SEQ, D_MODEL), 1.0),
        'ln_g': 1.0 + nrm(k[1], (DEPTH, D_MODEL), 0.02),
        'ln_b': nrm(k[2], (DEPTH, D_MODEL), 0.02),
        'pool_w_in': nrm(k[3], (nA, D_MODEL, 2 * D_POOL), D_MODEL ** -0.5) * pool_col,
        'pool_w_grp': nrm(k[4], (nA, N_POOL_GROUPS, POOL_GROUP, POOL_GROUP), POOL_GROUP ** -0.5),
        'pool_scale': 1.0 + nrm(k[5], (nA, D_POOL), 0.02),
        'pool_w_out': nrm(k[6], (nA, D_POOL, D_MODEL), D_POOL ** -0.5 * DN_BETA),
        'nsa_w_in': nrm(k[7], (nB, D_MODEL, D_NSA_IN), D_MODEL ** -0.5) * nsa_col,
        'nsa_cmp_pos_k': nrm(k[8], (nB, CMP_BLOCK, HEAD_DIM), 0.02),
        'nsa_cmp_w1_k': nrm(k[9], (nB, CMP_BLOCK * HEAD_DIM, CMP_HIDDEN), (CMP_BLOCK * HEAD_DIM) ** -0.5),
        'nsa_cmp_w2_k': nrm(k[10], (nB, CMP_HIDDEN, HEAD_DIM), CMP_HIDDEN ** -0.5),
        'nsa_cmp_pos_v': nrm(k[11], (nB, CMP_BLOCK, HEAD_DIM), 0.02),
        'nsa_cmp_w1_v': nrm(k[12], (nB, CMP_BLOCK * HEAD_DIM, CMP_HIDDEN), (CMP_BLOCK * HEAD_DIM) ** -0.5),
        'nsa_cmp_w2_v': nrm(k[13], (nB, CMP_HIDDEN, HEAD_DIM), CMP_HIDDEN ** -0.5),
        'nsa_w_out': nrm(k[14], (nB, D_ATT, D_MODEL), D_ATT ** -0.5 * DN_BETA),
    }

def first_block(x, ln_g, ln_b, pool_w_in, pool_w_grp, pool_scale, pool_w_out,
              nsa_w_in, nsa_cmp_pos_k, nsa_cmp_w1_k, nsa_cmp_w2_k,
              nsa_cmp_pos_v, nsa_cmp_w1_v, nsa_cmp_w2_v, nsa_w_out):
    for i in range(DEPTH):
        j = i // N_MIXERS
        if i % N_MIXERS == 0:
            y = pool_mixer(x, pool_w_in[j], pool_w_grp[j], pool_scale[j], pool_w_out[j])
        else:
            y = nsa_mixer(x, nsa_w_in[j], nsa_cmp_pos_k[j], nsa_cmp_w1_k[j], nsa_cmp_w2_k[j],
                          nsa_cmp_pos_v[j], nsa_cmp_w1_v[j], nsa_cmp_w2_v[j], nsa_w_out[j])
        x = layer_norm(DN_ALPHA * x + y, ln_g[i], ln_b[i])
    return x


CHUNK = 64

MIX_WIDTH = D_MODEL
CONV_W = MIX_WIDTH // 2
LRU_W = MIX_WIDTH - CONV_W
N_CONV_HEADS = 8
N_LRU_HEADS = 8
CONV_HD = CONV_W // N_CONV_HEADS
LRU_HD = LRU_W // N_LRU_HEADS
SHORT_CONV_K = 3
LRU_CONV_K = 4
LRU_C = 8.0
N_IN = 3 * CONV_W + 2 * LRU_W

PEER_HEADS = 8
PEER_TOPK = 16
N_KEYS = 128
N_EXPERTS = N_KEYS * N_KEYS
PEER_DK = 128
PEER_DK_HALF = PEER_DK // 2
PEER_BLOCK = 128

EPS = 1e-6


def rmsnorm(x, g):
    x32 = x.astype(jnp.float32)
    y = x32 * lax.rsqrt(jnp.mean(x32 * x32, axis=-1, keepdims=True) + EPS)
    return y.astype(x.dtype) * g

def head_rmsnorm(y, g, n_heads):
    b, s, w = y.shape
    yh = y.reshape(b, s, n_heads, w // n_heads).astype(jnp.float32)
    yh = yh * lax.rsqrt(jnp.mean(yh * yh, axis=-1, keepdims=True) + EPS)
    return yh.reshape(b, s, w).astype(y.dtype) * g

def modulate(h, shift, scale):
    return h * (1.0 + scale[:, None, :]) + shift[:, None, :]

def causal_dwconv(x, w):
    k_w = w.shape[0]
    s = x.shape[1]
    xp = jnp.pad(x, ((0, 0), (k_w - 1, 0), (0, 0)))
    out = xp[:, 0:s] * w[0]
    for k in range(1, k_w):
        out = out + xp[:, k:k + s] * w[k]
    return out

def rg_lru(xr, w_r, b_r, w_i, b_i, lam):
    b, s, _ = xr.shape
    xh = xr.reshape(b, s, N_LRU_HEADS, LRU_HD)
    r = jax.nn.sigmoid(jnp.einsum('bshi,hij->bshj', xh, w_r) + b_r).astype(jnp.float32)
    i = jax.nn.sigmoid(jnp.einsum('bshi,hij->bshj', xh, w_i) + b_i).astype(jnp.float32)
    log_a = -LRU_C * r * jax.nn.softplus(-lam.astype(jnp.float32))
    a = jnp.exp(log_a)
    u = jnp.sqrt(-jnp.expm1(2.0 * log_a)) * (i * xh.astype(jnp.float32))

    def combine(e1, e2):
        a1, b1 = e1
        a2, b2 = e2
        return a1 * a2, a2 * b1 + b2

    _, h = lax.associative_scan(combine, (a, u), axis=1)
    return h.reshape(b, s, LRU_W).astype(xr.dtype)

def peer(h, w_q, sub_keys, expert_u, expert_v):
    b, s, d = h.shape
    t = b * s
    hb = h.reshape(t // PEER_BLOCK, PEER_BLOCK, d)
    kk = PEER_TOPK * PEER_TOPK

    def block(xb):
        p = xb.shape[0]
        q = (xb @ w_q).reshape(p, PEER_HEADS, 2, PEER_DK_HALF)
        sc = jnp.einsum('phcd,hcnd->phcn', q, sub_keys).astype(jnp.float32)
        top_s, top_i = lax.top_k(sc, PEER_TOPK)
        cand_s = (top_s[:, :, 0, :, None] + top_s[:, :, 1, None, :]).reshape(p, PEER_HEADS, kk)
        cand_i = (top_i[:, :, 0, :, None] * N_KEYS + top_i[:, :, 1, None, :]).reshape(p, PEER_HEADS, kk)
        best_s, best_pos = lax.top_k(cand_s, PEER_TOPK)
        idx = jnp.take_along_axis(cand_i, best_pos, axis=-1)
        g = jax.nn.softmax(best_s, axis=-1)
        u_sel = expert_u[idx]
        act = jax.nn.gelu(jnp.einsum('phkd,pd->phk', u_sel, xb), approximate=False)
        coef = (g * act.astype(jnp.float32)).astype(xb.dtype)
        return jnp.einsum('phk,phkd->pd', coef, expert_v[idx])

    return lax.map(block, hb).reshape(b, s, d)

def second_inputs(seed: int = 0) -> dict:
    key = jax.random.key(seed)
    ks = jax.random.split(key, 24)
    f32 = jnp.float32
    L = DEPTH

    def nrm(k, shape, scale):
        return jax.random.normal(k, shape, f32) * scale

    a8 = jax.random.uniform(ks[13], (L, N_LRU_HEADS, LRU_HD), f32, 0.9, 0.999)
    a_base = a8 ** (1.0 / LRU_C)
    lru_lambda = jnp.log(a_base) - jnp.log1p(-a_base)

    return {
        "x": nrm(ks[0], (BATCH, SEQ, D_MODEL), 1.0),
        "c": nrm(ks[1], (BATCH, D_MODEL), 1.0),
        "w_ada": nrm(ks[2], (L, D_MODEL, 6 * D_MODEL), 0.5 * D_MODEL ** -0.5),
        "b_ada": nrm(ks[3], (L, 6 * D_MODEL), 0.02),
        "norm1_g": 1.0 + nrm(ks[4], (L, D_MODEL), 0.02),
        "w_in": nrm(ks[5], (L, D_MODEL, N_IN), D_MODEL ** -0.5),
        "conv_a_w": nrm(ks[6], (L, SHORT_CONV_K, CONV_W), SHORT_CONV_K ** -0.5),
        "conv_b_w": nrm(ks[7], (L, LRU_CONV_K, LRU_W), LRU_CONV_K ** -0.5),
        "conv_b_b": nrm(ks[8], (L, LRU_W), 0.02),
        "w_r": nrm(ks[9], (L, N_LRU_HEADS, LRU_HD, LRU_HD), LRU_HD ** -0.5),
        "b_r": nrm(ks[10], (L, N_LRU_HEADS, LRU_HD), 0.02),
        "w_i": nrm(ks[11], (L, N_LRU_HEADS, LRU_HD, LRU_HD), LRU_HD ** -0.5),
        "b_i": nrm(ks[12], (L, N_LRU_HEADS, LRU_HD), 0.02),
        "lru_lambda": lru_lambda,
        "gn_a": 1.0 + nrm(ks[14], (L, CONV_W), 0.02),
        "gn_b": 1.0 + nrm(ks[15], (L, LRU_W), 0.02),
        "w_out": nrm(ks[16], (L, MIX_WIDTH, D_MODEL), MIX_WIDTH ** -0.5),
        "norm2_g": 1.0 + nrm(ks[17], (L, D_MODEL), 0.02),
        "w_q": nrm(ks[18], (L, D_MODEL, PEER_HEADS * PEER_DK), D_MODEL ** -0.5),
        "sub_keys": nrm(ks[19], (L, PEER_HEADS, 2, N_KEYS, PEER_DK_HALF), PEER_DK_HALF ** -0.5),
        "expert_u": nrm(ks[20], (L, N_EXPERTS, D_MODEL), D_MODEL ** -0.5),
        "expert_v": nrm(ks[21], (L, N_EXPERTS, D_MODEL), PEER_HEADS ** -0.5),
        "final_g": 1.0 + nrm(ks[22], (D_MODEL,), 0.02),
    }

def second_block(x, c, w_ada, b_ada, norm1_g, w_in, conv_a_w, conv_b_w, conv_b_b,
              w_r, b_r, w_i, b_i, lru_lambda, gn_a, gn_b, w_out,
              norm2_g, w_q, sub_keys, expert_u, expert_v, final_g):
    c_act = jax.nn.silu(c)
    for l in range(DEPTH):
        ada = c_act @ w_ada[l] + b_ada[l]
        sh1, sc1, g1, sh2, sc2, g2 = jnp.split(ada, 6, axis=-1)

        h = modulate(rmsnorm(x, norm1_g[l]), sh1, sc1)
        z = h @ w_in[l]
        gate_b, gate_c, xa, xr, gr = jnp.split(
            z, [CONV_W, 2 * CONV_W, 3 * CONV_W, 3 * CONV_W + LRU_W], axis=-1)

        y_a = gate_b * causal_dwconv(gate_c * xa, conv_a_w[l])

        xr = causal_dwconv(xr, conv_b_w[l]) + conv_b_b[l]
        y_b = rg_lru(xr, w_r[l], b_r[l], w_i[l], b_i[l], lru_lambda[l]) * jax.nn.gelu(gr)

        y = jnp.concatenate([head_rmsnorm(y_a, gn_a[l], N_CONV_HEADS),
                             head_rmsnorm(y_b, gn_b[l], N_LRU_HEADS)], axis=-1) @ w_out[l]
        x = x + g1[:, None, :] * y

        h = modulate(rmsnorm(x, norm2_g[l]), sh2, sc2)
        x = x + g2[:, None, :] * peer(h, w_q[l], sub_keys[l], expert_u[l], expert_v[l])

    return rmsnorm(x, final_g)


def setup_inputs(seed=0):
    out = dict(first_inputs(seed))
    for name, value in second_inputs(seed + 1).items():
        if name != "x":
            out[name + "_2"] = value
    return out


def reference(
    x, ln_g, ln_b, pool_w_in, pool_w_grp, pool_scale, pool_w_out, nsa_w_in, nsa_cmp_pos_k,
    nsa_cmp_w1_k, nsa_cmp_w2_k, nsa_cmp_pos_v, nsa_cmp_w1_v, nsa_cmp_w2_v, nsa_w_out, c_2,
    w_ada_2, b_ada_2, norm1_g_2, w_in_2, conv_a_w_2, conv_b_w_2, conv_b_b_2, w_r_2, b_r_2,
    w_i_2, b_i_2, lru_lambda_2, gn_a_2, gn_b_2, w_out_2, norm2_g_2, w_q_2, sub_keys_2,
    expert_u_2, expert_v_2, final_g_2,
):
    x = first_block(
        x, ln_g, ln_b, pool_w_in, pool_w_grp, pool_scale, pool_w_out, nsa_w_in, nsa_cmp_pos_k,
        nsa_cmp_w1_k, nsa_cmp_w2_k, nsa_cmp_pos_v, nsa_cmp_w1_v, nsa_cmp_w2_v, nsa_w_out,
    )
    return second_block(
        x, c_2, w_ada_2, b_ada_2, norm1_g_2, w_in_2, conv_a_w_2, conv_b_w_2, conv_b_b_2, w_r_2,
        b_r_2, w_i_2, b_i_2, lru_lambda_2, gn_a_2, gn_b_2, w_out_2, norm2_g_2, w_q_2,
        sub_keys_2, expert_u_2, expert_v_2, final_g_2,
    )


_drawn_inputs = setup_inputs


def setup_inputs(seed=0):
    import zlib

    import numpy as np

    out = dict(_drawn_inputs(seed))
    spreads = {}
    factors = {'pool_scale': 8.0,
     'norm1_g_2': 5.534,
     'conv_b_b_2': 3.409,
     'b_r_2': 21.672,
     'b_i_2': 8.0,
     'gn_a_2': 52.439,
     'gn_b_2': 59.463,
     'norm2_g_2': 25.721,
     'final_g_2': 25.55}
    for name, (base, spread) in spreads.items():
        noise = np.random.default_rng([zlib.crc32(name.encode()), seed]).standard_normal(out[name].shape)
        drawn = base * np.exp(spread * noise) if base else spread * noise
        out[name] = __import__('jax').numpy.asarray(drawn.astype(out[name].dtype))
    for name, factor in factors.items():
        out[name] = (out[name] * factor).astype(out[name].dtype)
    return out
```

```python
import concourse.bass as bass
from concourse import mybir
from contextlib import ExitStack

P = 128
T = 512
NT = T // P
DM = 1024
KD = DM // P
WINDOWS = (2, 4, 8, 16)
NG = len(WINDOWS)
GC = 4
PAD = 16
NKP = NG * GC
ADA_W = 256
ADA_PER_G = 6
NADA = NG * ADA_PER_G
ADA_RING = 4
NJ = 4
XR, GR, GCT, XA, GB = range(5)
HEADS = 8
TOPK = 16
NKEYS = 128
DKH = 64
RING = 8
STEPS = NT * HEADS
BATCH = 2
LN_EPS = 1e-5
EPS = 1e-6
ALPHA = 2.0 ** 0.25
LOWEST = -3.0e38
C_C, C_SCALE = 0, 8
C_CONVA, C_CONVB = 24, 36
C_CBB, C_BR, C_BI, C_LAM, C_GNA, C_GNB, NPAR = 52, 56, 60, 64, 68, 72, 76


def mixers_and_peer(nc, x, xT, par, ln_g, ln_b, w_in, w_grp, w_out, w_ada, b_ada, norm1, w_in2,
                    w_r, w_i, w_out2, norm2, w_q, keysT, experts, final_g, out):
    f32, u32 = mybir.dt.float32, mybir.dt.uint32
    ALU, ACT, AX = mybir.AluOpType, mybir.ActivationFunctionType, mybir.AxisListType

    with ExitStack() as ctx:
        def sb(name, shape, dt=f32):
            return ctx.enter_context(nc.sbuf_tensor(name, shape, dt))

        def sem(name):
            return ctx.enter_context(nc.semaphore(name))

        xres = sb("xres", [P, NT, DM])
        ada = sb("ada", [P, 6, DM])
        lnw = sb("lnw", [P, 2, DM])
        ident = sb("ident", [P, P])
        ones = sb("ones", [P, P])
        headmean = sb("headmean", [P, P])
        pars = sb("pars", [P, NPAR])
        cact = sb("cact", [P, KD])
        invcnt = sb("invcnt", [P, PAD])
        stats = sb("stats", [P, 16])
        lrate = sb("lrate", [P, NJ])
        lscr = sb("lscr", [P, 2, NJ])

        KB = 256
        arena = sb("arena", [P, 156 * KB + 128])

        def view(kb, n):
            at = int(kb * KB)
            return arena[:, at:at + n]

        xT_s = view(0, KD * T).rearrange("p (k t) -> p k t", k=KD)
        upad = view(16, GC * (PAD + T)).rearrange("p (c t) -> p c t", c=GC)
        wa = view(24.25, PAD + T)
        wb = view(26.3125, PAD + T)
        pooled = view(28.375, GC * T).rearrange("p (c t) -> p c t", c=GC)
        zs = view(36.375, GC * T).rearrange("p (c t) -> p c t", c=GC)
        wgrp = view(44.375, GC * T).rearrange("p (c d) -> p c d", c=GC)
        inring = view(52.375, 8 * DM).rearrange("p (s k f) -> p s k f", s=8, k=KD)
        adaring = view(84.375, ADA_RING * KD * ADA_W).rearrange("p (r k f) -> p r k f", r=ADA_RING, k=KD)
        yin = view(116.375, NKP * T).rearrange("p (c t) -> p c t", c=NKP)
        adaacc = view(148.375, 2 * ADA_W).rearrange("p (a f) -> p a f", a=2)
        ntmp = view(150.375, DM)
        wout0 = view(84.375, NKP * T).rearrange("p (k f) -> p k f", k=NKP)
        wout1 = view(52.375, NKP * T).rearrange("p (k f) -> p k f", k=NKP)
        h1tmp = view(36.375, 2 * DM).rearrange("p (a f) -> p a f", a=2)
        h1T = view(0, KD * T).rearrange("p (k t) -> p k t", k=KD)
        in2 = view(16, 5 * DM).rearrange("p (s k f) -> p s k f", s=5, k=KD)
        yT = view(36.375, 2 * NJ * T).rearrange("p (k t) -> p k t", k=2 * NJ)
        wout2 = view(52.375, KD * DM).rearrange("p (k f) -> p k f", k=KD)
        wq = view(84.375, KD * DM).rearrange("p (k f) -> p k f", k=KD)
        tmp = [view(116.375 + 2.015625 * i, T + 4) for i in range(15)]
        xrp, cx, rt, iu, den, aa, om, hh, gg, gcs, vp, ya, sqa, sqb, rn = tmp
        bdr = view(148.375, NJ * P).rearrange("p (j f) -> p j f", j=NJ)
        bdi = view(150.375, NJ * P).rearrange("p (j f) -> p j f", j=NJ)
        keys = view(152.375, HEADS * NKEYS).rearrange("p (h n) -> p h n", h=HEADS)
        xtmp = view(116.375, DM)
        h2 = view(0, NT * DM).rearrange("p (t f) -> p t f", t=NT)
        ring = view(16, RING * 2 * DM).rearrange("p (r f) -> p r f", r=RING)
        scores = view(116.375, (STEPS + 1) * 2 * NKEYS).rearrange("p (s n) -> p s n", s=STEPS + 1)
        diag = view(84.375, RING * P).rearrange("p (r f) -> p r f", r=RING)
        outb = view(88.375, DM)
        zeros = view(92.375, P)
        cur = view(80.0, 2 * NKEYS).rearrange("p (c n) -> p c n", c=2)
        cand = view(81.0, TOPK * TOPK).rearrange("p (a b) -> p a b", a=TOPK)
        hot = view(82.0, TOPK * 2 * TOPK).rearrange("p (k c a) -> p k c a", k=TOPK, c=2)
        rest = view(149.5, 2 * NKEYS)
        gate, dots, acts = (view(151.5 + 0.125 * i, 2 * TOPK).rearrange("p (e n) -> p e n", e=2) for i in range(3))
        idxf = view(151.875, TOPK)
        h2cur = ada[:, 2, :]
        qT = ada[:, 4, :].rearrange("p (a t) -> p a t", a=2)
        fing = ada[:, 3, :]

        def h2T_of(k):
            return lnw[:, k // 2, (k % 2) * T:(k % 2 + 1) * T] if k < 4 else \
                ada[:, (k - 4) // 2, (k % 2) * T:(k % 2 + 1) * T]

        topv = sb("topv", [P, 2, TOPK])
        topi = sb("topi", [P, 2, TOPK], u32)
        topf = sb("topf", [P, 2, TOPK])
        best = sb("best", [P, TOPK])
        bpos = sb("bpos", [P, TOPK], u32)
        ab = sb("ab", [P, TOPK, 2], u32)
        abf = sb("abf", [P, TOPK, 2])
        iota16 = sb("iota16", [P, TOPK])
        top1 = sb("top1", [P, 1])
        esum = sb("esum", [P, 1])
        idx = sb("idx", [P, 2, TOPK], u32)

        ps = [ctx.enter_context(nc.psum_tensor(f"ps{i}", [P, T], f32)) for i in range(8)]

        par_in, xT_in, bada_in, x_in, ln_in = map(sem, ("par_in", "xT_in", "bada_in", "x_in", "ln_in"))
        in_arr = [sem(f"in_arr{s}") for s in range(8)]
        grp_arr, ntmp_in = sem("grp_arr"), sem("ntmp_in")
        ada_arr = [sem(f"ada_arr{r}") for r in range(ADA_RING)]
        wout_arr = [sem(f"wout_arr{i}") for i in range(4)]
        in2_arr = [sem(f"in2_arr{s}") for s in range(5)]
        bd_in, keys_in, wout2_in, wq_in, fing_in = map(sem, ("bd_in", "keys_in", "wout2_in", "wq_in", "fing_in"))
        consts = sem("consts")
        vconsts = sem("vconsts")
        cact_ready = sem("cact_ready")
        in_mm = sem("in_mm")
        u_ready = sem("u_ready")
        z_ready = sem("z_ready")
        m_ready = sem("m_ready")
        grp_mm = sem("grp_mm")
        yin_ready = sem("yin_ready")
        acc_ready = sem("acc_ready")
        acc_mm = sem("acc_mm")
        ada_used = sem("ada_used")
        ada_added = sem("ada_added")
        yout_mm = sem("yout_mm")
        h1_ready, h1_tr, h1T_ready = sem("h1_ready"), sem("h1_tr"), sem("h1T_ready")
        lam_exp, lam_one, lam_ln, lrate_ready = map(sem, ("lam_exp", "lam_one", "lam_ln", "lrate_ready"))
        bd_zero = sem("bd_zero")
        pads2 = sem("pads2")
        in2_mm = sem("in2_mm")
        gates_mm = sem("gates_mm")
        norm_mm = sem("norm_mm")
        xr_copied, gg_ready, gc_copied, sig_ready, sq_ready = map(
            sem, ("xr_copied", "gg_ready", "gc_copied", "sig_ready", "sq_ready"))
        cx_ready, yb_ready, ya_ready, yT_ready = map(sem, ("cx_ready", "yb_ready", "ya_ready", "yT_ready"))
        v_ready = sem("v_ready")
        tanh_ready = sem("tanh_ready")
        om_ready, om_root = sem("om_ready"), sem("om_root")
        var_ready, root_ready = sem("var_ready"), sem("root_ready")
        rn_ready = sem("rn_ready")
        y2_mm, y2_read, h2_ready, h2_tr, h2T_ready = map(
            sem, ("y2_mm", "y2_read", "h2_ready", "h2_tr", "h2T_ready"))
        q_mm, q_copied, score_mm, score_ready = map(sem, ("q_mm", "q_copied", "score_mm", "score_ready"))
        arr = [sem(f"arr{r}") for r in range(RING)]
        slot_free = sem("slot_free")
        pool_go = sem("pool_go")
        vec_go = sem("vec_go")
        cur_ready, best_ready, exp_ready, idx_ready = map(sem, ("cur_ready", "best_ready", "exp_ready", "idx_ready"))
        dots_done, gelu_done, diag_ready = map(sem, ("dots_done", "gelu_done", "diag_ready"))
        tile_mm, tile_read = sem("tile_mm"), sem("tile_read")
        out_ready, out_stored, outb_free = sem("out_ready"), sem("out_stored"), sem("outb_free")

        block = ctx.enter_context(nc.Block())

        def row_on_all(row):
            return row.rearrange("(a n) -> a n", a=1).to_broadcast([P, DM])

        @block.sync
        def _(sp):
            def load_in(g, s):
                if g:
                    sp.wait_ge(in_mm, 8 * (g - 1) + s + 1)
                sp.dma_start(inring[:, s, :, :].rearrange("p k f -> p (k f)"), w_in[g, s, :, :]).then_inc(in_arr[s], 16)

            def load_ada(b):
                if b >= ADA_RING:
                    sp.wait_ge(ada_used, b - ADA_RING + 1)
                sp.dma_start(adaring[:, b % ADA_RING, :, :].rearrange("p k f -> p (k f)"),
                             w_ada[b, :, :]).then_inc(ada_arr[b % ADA_RING], 16)

            def load_grp(g):
                if g:
                    sp.wait_ge(grp_mm, GC * g)
                sp.dma_start(wgrp.rearrange("p c d -> p (c d)"), w_grp[g, :, :]).then_inc(grp_arr, 16)

            sp.dma_start(pars[:, :], par).then_inc(par_in, 16)
            load_in(0, 0)
            for k in range(0, KD, 2):
                sp.dma_start(xT_s[:, k:k + 2, :], xT[k * P:(k + 2) * P, :].rearrange("(k p) t -> p k t", p=P)).then_inc(xT_in, 16)
            load_in(0, 1)
            load_ada(0)
            load_in(0, 2)
            load_in(0, 3)
            for b in range(1, ADA_RING):
                load_ada(b)
            for s in range(4, 8):
                load_in(0, s)
            load_grp(0)
            for n in range(6):
                sp.dma_start(ada[:, n, :], row_on_all(b_ada[n * DM:(n + 1) * DM])).then_inc(bada_in, 16)
            sp.dma_start(ntmp, row_on_all(norm1)).then_inc(ntmp_in, 16)
            for g in range(1, NG):
                for s in range(8):
                    load_in(g, s)
                    if s < ADA_PER_G:
                        load_ada(ADA_PER_G * (g - 1) + s + ADA_RING)
                load_grp(g)
                if g == 1:
                    for t in range(NT):
                        sp.dma_start(xres[:, t, :], x[t * P:(t + 1) * P, :]).then_inc(x_in, 16)
                    sp.dma_start(lnw[:, 0, :], row_on_all(ln_g)).then_inc(ln_in, 16)
                    sp.dma_start(lnw[:, 1, :], row_on_all(ln_b)).then_inc(ln_in, 16)
                if g == 2:
                    sp.wait_ge(ada_added, 8)
                    sp.dma_start(ntmp, row_on_all(norm2)).then_inc(ntmp_in, 16)
            for b in range(ADA_PER_G * (NG - 1) + ADA_RING, NADA):
                load_ada(b)
            sp.wait_ge(ada_used, NADA)
            for i in range(2):
                sp.dma_start(wout0[:, 8 * i:8 * i + 8, :].rearrange("p k f -> p (k f)"),
                             w_out[0, :, 8 * i * T:(8 * i + 8) * T]).then_inc(wout_arr[i], 16)
            sp.wait_ge(in_mm, 8 * NG)
            for i in range(2):
                sp.dma_start(wout1[:, 8 * i:8 * i + 8, :].rearrange("p k f -> p (k f)"),
                             w_out[1, :, 8 * i * T:(8 * i + 8) * T]).then_inc(wout_arr[2 + i], 16)

            sp.wait_ge(grp_mm, GC * NG)
            for s in range(5):
                sp.dma_start(in2[:, s, :, :].rearrange("p k f -> p (k f)"), w_in2[0, s, :, :]).then_inc(in2_arr[s], 16)
            sp.wait_ge(ada_added, NADA)
            sp.dma_start(keys.rearrange("p h n -> p (h n)"), keysT).then_inc(keys_in, 16)
            sp.wait_ge(bd_zero, 2)
            for e in range(2):
                r = slice(64 * e, 64 * e + 64)
                sp.dma_start(bdr[r, :, r], w_r[e, :, :, :]).then_inc(bd_in, 16)
                sp.dma_start(bdi[r, :, r], w_i[e, :, :, :]).then_inc(bd_in, 16)
            sp.wait_ge(yout_mm, NT)
            sp.dma_start(wq.rearrange("p k f -> p (k f)"), w_q).then_inc(wq_in, 16)
            sp.wait_ge(yout_mm, 2 * NT)
            sp.dma_start(wout2.rearrange("p k f -> p (k f)"), w_out2).then_inc(wout2_in, 16)
            for j in range(1, NJ):
                for s in range(5):
                    sp.wait_ge(in2_mm, 5 * (j - 1) + s + 1)
                    sp.dma_start(in2[:, s, :, :].rearrange("p k f -> p (k f)"), w_in2[j, s, :, :]).then_inc(in2_arr[s], 16)
            sp.wait_ge(h2_ready, NT)
            sp.dma_start(fing, row_on_all(final_g)).then_inc(fing_in, 16)
            with sp.Fori(0, NT, 1) as t:
                sp.wait_ge(out_ready, t + 1)
                sp.dma_start(out[bass.ds(t * P, P), :], outb).then_inc(out_stored, 16)
                sp.wait_ge(out_stored, 16 * t + 16)
                sp.sem_inc(outb_free, 1)

        @block.gpsimd
        def _(pool):
            nc.gpsimd.memset(ident[:, :], 0.0).then_inc(consts, 1)
            nc.gpsimd.memset(ones[:, :], 1.0).then_inc(consts, 1)
            nc.gpsimd.iota(iota16[:, :], pattern=[[1, TOPK]], base=0, channel_multiplier=0,
                           allow_small_or_imprecise_dtypes=True).then_inc(consts, 1)
            nc.gpsimd.iota(invcnt[:, :], pattern=[[1, PAD]], base=1, channel_multiplier=0,
                           allow_small_or_imprecise_dtypes=True).then_inc(consts, 1)
            pool.wait_ge(consts, 4)
            nc.gpsimd.affine_select(out=ident[:, :], in_=ident[:, :], compare_op=ALU.not_equal, fill=1.0,
                                    base=0, pattern=[[-1, P]], channel_multiplier=1).then_inc(consts, 1)
            pool.wait_ge(ada_added, NADA)
            nc.gpsimd.memset(bdr, 0.0).then_inc(bd_zero, 1)
            nc.gpsimd.memset(bdi, 0.0).then_inc(bd_zero, 1)
            with pool.Fori(0, STEPS // 2, 1) as i:
                for e in range(2):
                    pool.wait_ge(idx_ready, 2 * i + e + 1)
                    pool.sem_inc(pool_go, 1)
                    for n in range(TOPK):
                        pool.wait_ge(slot_free, 2 * TOPK * i + TOPK * e + n + 1)
                        pool.sem_inc(pool_go, 1)
                        nc.gpsimd.indirect_dma_start(
                            ring[:, n % RING, :], None, experts,
                            bass.IndirectOffsetOnAxis(ap=idx[:, e, n:n + 1], axis=0)).then_inc(arr[n % RING], 16)

        @block.tensor
        def _(pe):
            mm = nc.tensor.matmul

            pe.sem_inc(yin_ready, GC)
            pe.sem_inc(z_ready, GC)
            pe.wait_ge(xT_in, 16 * KD // 2)
            pe.wait_ge(consts, 5)
            pe.wait_ge(vconsts, 1)
            with pe.Fori(0, NG, 1) as g:
                def ada_sum(i):
                    pe.wait_ge(acc_ready, ADA_PER_G * g + i + 1)
                    if i < GC:
                        pe.wait_ge(z_ready, GC * g + i + 1)
                    else:
                        pe.wait_ge(ada_added, ADA_PER_G * g + i - 1)
                    bank = GC + i if i < GC else GC + i - 2
                    mm(ps[bank][:, 0:ADA_W], lhsT=ones[:, :], rhs=adaacc[:, i % 2, :],
                       start=True, stop=True).then_inc(acc_mm, 1)

                for s in range(2 * GC):
                    pe.wait_ge(in_arr[s], 16 * g + 16)
                    if s < GC:
                        pe.wait_ge(yin_ready, GC * g + s + 1)
                    else:
                        k = s - GC
                        pe.wait_ge(ada_added, ADA_PER_G * g + (k + 1 if k < 2 else k + 3))
                    for k in range(KD):
                        last = mm(ps[s][:, :], lhsT=inring[:, s, k, :], rhs=xT_s[:, k, :],
                                  start=(k == 0), stop=(k == KD - 1))
                    last.then_inc(in_mm, 1)
                    if s < 4:
                        ada_sum(s)
                    if s == 4:
                        ada_sum(4)
                        ada_sum(5)
                pe.wait_ge(m_ready, GC * g + GC)
                pe.wait_ge(grp_arr, 16 * g + 16)
                for d in range(GC):
                    for c in range(GC):
                        last = mm(ps[d][:, :], lhsT=wgrp[:, c, d * P:(d + 1) * P], rhs=pooled[:, c, :],
                                  start=(c == 0), stop=(c == GC - 1))
                    last.then_inc(grp_mm, 1)

            pe.wait_ge(yin_ready, GC + NKP)
            pe.wait_ge(ada_added, NADA)
            for half, w in ((0, wout0), (1, wout1)):
                for t in range(NT):
                    for k in range(NKP):
                        if t == 0 and k % 8 == 0:
                            pe.wait_ge(wout_arr[2 * half + k // 8], 16)
                        last = mm(ps[4 * half + t][:, :], lhsT=yin[:, k, t * P:(t + 1) * P], rhs=w[:, k, :],
                                  start=(k == 0), stop=(k == NKP - 1))
                    last.then_inc(yout_mm, 1)

            for t in range(NT):
                pe.wait_ge(h1_ready, t + 1)
                for k in range(KD):
                    bank = ps[t] if k < 4 else ps[4 + t]
                    last = nc.tensor.transpose(bank[:, (k % 4) * P:(k % 4 + 1) * P],
                                               h1tmp[:, t % 2, k * P:(k + 1) * P], ident[:, :])
                last.then_inc(h1_tr, 1)

            def head_means(n):
                pe.wait_ge(sq_ready, n + 1)
                if n:
                    pe.wait_ge(rn_ready, n)
                mm(ps[7][:, :], lhsT=headmean[:, :], rhs=(sqb if n % 2 == 0 else sqa)[:, 0:T],
                   start=True, stop=True).then_inc(norm_mm, 1)

            pe.wait_ge(h1T_ready, 2 * NT)
            pe.wait_ge(bd_in, 64)
            read_by = {XR: xr_copied, GR: gg_ready, GCT: gc_copied, XA: v_ready, GB: ya_ready}
            for j in range(NJ):
                for s in range(5):
                    pe.wait_ge(in2_arr[s], 16 * (j + 1))
                    if j:
                        pe.wait_ge(read_by[s], j)
                    for k in range(KD):
                        last = mm(ps[s][:, :], lhsT=in2[:, s, k, :], rhs=h1T[:, k, :],
                                  start=(k == 0), stop=(k == KD - 1))
                    last.then_inc(in2_mm, 1)
                    if j and s == XR:
                        head_means(2 * j - 2)
                    if j and s == GR:
                        head_means(2 * j - 1)
                    if s == GCT:
                        pe.wait_ge(cx_ready, j + 1)
                        if j:
                            pe.wait_ge(sig_ready, 2 * j)
                        mm(ps[5][:, :], lhsT=bdr[:, j, :], rhs=cx[:, 0:T], start=True, stop=True).then_inc(gates_mm, 1)
                        mm(ps[6][:, :], lhsT=bdi[:, j, :], rhs=cx[:, 0:T], start=True, stop=True).then_inc(gates_mm, 1)
            head_means(2 * NJ - 2)
            head_means(2 * NJ - 1)

            pe.wait_ge(yT_ready, 2 * NJ)
            pe.wait_ge(wout2_in, 16)
            for t in range(NT):
                for half in range(2):
                    for k in range(KD):
                        last = mm(ps[2 * t + half][:, :], lhsT=yT[:, k, t * P:(t + 1) * P],
                                  rhs=wout2[:, k, half * T:(half + 1) * T], start=(k == 0), stop=(k == KD - 1))
                    last.then_inc(y2_mm, 1)
            pe.sem_inc(slot_free, RING)

            def transpose_h2(t):
                pe.wait_ge(h2_ready, t + 1)
                for k in range(KD):
                    last = nc.tensor.transpose(ps[2 * t + k // 4][:, (k % 4) * P:(k % 4 + 1) * P],
                                               h2[:, t, k * P:(k + 1) * P], ident[:, :])
                last.then_inc(h2_tr, 1)

            def query(h, t0, t1, bank):
                for k in range(KD):
                    last = mm(ps[bank][:, 0:(t1 - t0) * P], lhsT=wq[:, k, h * P:(h + 1) * P],
                              rhs=h2T_of(k)[:, t0 * P:t1 * P], start=(k == 0), stop=(k == KD - 1))
                last.then_inc(q_mm, 1)

            def score(h, t0, t1, bank):
                for t in range(t0, t1):
                    for c in range(2):
                        r = slice(DKH * c, DKH * c + DKH)
                        last = mm(ps[bank + c][:, (t - t0) * NKEYS:(t - t0 + 1) * NKEYS],
                                  lhsT=qT[r, h % 2, t * P:(t + 1) * P], rhs=keys[r, h, :], start=True, stop=True)
                last.then_inc(score_mm, 1)

            transpose_h2(0)
            pe.wait_ge(wq_in, 16)
            pe.wait_ge(keys_in, 16)
            pe.wait_ge(h2T_ready, 2)
            pe.wait_ge(y2_read, NT)
            for h in range(HEADS + 1):
                if h < HEADS:
                    query(h, 0, 1, h % 2)
                if h:
                    pe.wait_ge(q_copied, h)
                    if h > 2:
                        pe.wait_ge(score_ready, 2 * (h - 2))
                    score(h - 1, 0, 1, 2 + 2 * ((h - 1) % 2))
            for t in range(1, NT):
                if t == 1:
                    pe.wait_ge(score_ready, 2 * HEADS)
                transpose_h2(t)
            pe.wait_ge(h2T_ready, 2 * NT)
            for h in range(HEADS + 1):
                if h < HEADS:
                    query(h, 1, NT, 2 + h % 2)
                if h:
                    pe.wait_ge(q_copied, HEADS + h)
                    if h > 2:
                        pe.wait_ge(score_ready, 2 * (HEADS + h - 2))
                    score(h - 1, 1, NT, 4 + 2 * ((h - 1) % 2))

            pe.sem_inc(tile_read, 1)
            pe.wait_ge(vconsts, 2)
            zero_rows = ident[:, :].unsqueeze(1).to_broadcast([P, 4, P])
            with pe.Fori(0, NT, 1) as t:
                pe.wait_ge(tile_read, t + 1)
                for half in range(2):
                    mm(ps[half][:, :].rearrange("p (a b) -> p a b", a=4), lhsT=zeros, rhs=zero_rows, start=True, stop=False)
                with pe.Fori(0, HEADS // 2, 1) as i:
                    for e in range(2):
                        for n in range(TOPK):
                            pe.wait_ge(diag_ready, t * (HEADS * TOPK) + i * (2 * TOPK) + TOPK * e + n + 1)
                            for half in range(2):
                                last = mm(ps[half][:, :], lhsT=diag[:, n % RING, :],
                                          rhs=ring[:, n % RING, DM + half * T:DM + (half + 1) * T],
                                          start=False, stop=False)
                            last.then_inc(slot_free, 1)
                for half in range(2):
                    last = mm(ps[half][:, :].rearrange("p (a b) -> p a b", a=4), lhsT=zeros, rhs=zero_rows, start=False, stop=True)
                last.then_inc(tile_mm, 1)

        @block.scalar
        def _(act):
            act.wait_ge(par_in, 16)
            nc.scalar.activation(cact[:, :], pars[:, C_C:C_C + KD], ACT.Silu).then_inc(cact_ready, 1)
            act.wait_ge(lam_one, 1)
            nc.scalar.activation(lscr[:, 0, :], lscr[:, 0, :], ACT.Exp, scale=-1.0).then_inc(lam_exp, 1)
            act.wait_ge(lam_one, 2)
            nc.scalar.activation(lscr[:, 0, :], lscr[:, 0, :], ACT.Ln).then_inc(lam_ln, 1)
            act.wait_ge(vconsts, 1)

            for g in range(NG):
                for s in range(GC):
                    act.wait_ge(in_mm, 8 * g + s + 1)
                    if g:
                        act.wait_ge(m_ready, GC * (g - 1) + s + 1)
                    nc.scalar.copy(upad[:, s, PAD:], ps[s][:, :]).then_inc(u_ready, 1)
                for s in range(GC):
                    act.wait_ge(in_mm, 8 * g + GC + s + 1)
                    if g:
                        act.wait_ge(yin_ready, GC * g + s + 1)
                    nc.scalar.activation(zs[:, s, :], ps[GC + s][:, :], ACT.Silu).then_inc(z_ready, 1)

            def root(col, nth):
                act.wait_ge(var_ready, nth)
                nc.scalar.activation(stats[:, col:col + 1], stats[:, col:col + 1], ACT.Sqrt).then_inc(root_ready, 1)

            for t in range(NT + 1):
                if t < NT:
                    root(13, 2 * t + 1)
                    root(14, 2 * t + 2)
                if t:
                    act.wait_ge(h1_tr, t)
                    for b in range(2):
                        nc.scalar.copy(h1T[:, 4 * b:4 * b + 4, (t - 1) * P:t * P],
                                       ps[4 * b + t - 1][:, :].rearrange("p (k f) -> p k f", k=4)).then_inc(h1T_ready, 1)

            act.wait_ge(lrate_ready, 1)
            act.wait_ge(pads2, 1)

            def head_root(n):
                act.wait_ge(norm_mm, n + 1)
                if n:
                    act.wait_ge(yT_ready, n)
                nc.scalar.activation(rn[:, 0:T], ps[7][:, :], ACT.Sqrt, bias=stats[:, 15:16]).then_inc(rn_ready, 1)

            for j in range(NJ):
                act.wait_ge(in2_mm, 5 * j + XR + 1)
                nc.scalar.copy(xrp[:, 3:3 + T], ps[XR][:, :]).then_inc(xr_copied, 1)
                if j:
                    head_root(2 * j - 2)
                act.wait_ge(in2_mm, 5 * j + GR + 1)
                if j:
                    act.wait_ge(yT_ready, 2 * j - 1)
                nc.scalar.activation(gg[:, 0:T], ps[GR][:, :], ACT.Gelu).then_inc(gg_ready, 1)
                if j:
                    head_root(2 * j - 1)
                act.wait_ge(in2_mm, 5 * j + GCT + 1)
                nc.scalar.copy(gcs[:, 0:T], ps[GCT][:, :]).then_inc(gc_copied, 1)
                for n, (dst, bias) in enumerate(((rt, C_BR), (iu, C_BI))):
                    act.wait_ge(gates_mm, 2 * j + n + 1)
                    nc.scalar.activation(dst[:, 0:T], ps[5 + n][:, :], ACT.Sigmoid,
                                         bias=pars[:, bias + j:bias + j + 1]).then_inc(sig_ready, 1)
                act.drain()
                nc.scalar.activation(rt[:, 0:T], rt[:, 0:T], ACT.Tanh,
                                     scale=lrate[:, j:j + 1]).then_inc(tanh_ready, 1)
                act.wait_ge(om_ready, j + 1)
                nc.scalar.activation(om[:, 0:T], om[:, 0:T], ACT.Sqrt).then_inc(om_root, 1)
                act.wait_ge(yb_ready, j + 1)
                if j:
                    act.wait_ge(norm_mm, 2 * j - 1)
                nc.scalar.activation(sqb[:, 0:T], gg[:, 0:T], ACT.Square).then_inc(sq_ready, 1)
                act.wait_ge(ya_ready, j + 1)
                if j:
                    act.wait_ge(norm_mm, 2 * j)
                nc.scalar.activation(sqa[:, 0:T], ya[:, 0:T], ACT.Square).then_inc(sq_ready, 1)

            head_root(2 * NJ - 2)
            head_root(2 * NJ - 1)
            for t in range(NT):
                root(14, 2 * NT + t + 1)

            def copy_h2T(t):
                act.wait_ge(h2_tr, t + 1)
                for b in range(2):
                    dst = lnw if b == 0 else ada
                    nc.scalar.copy(dst[:, 0:2, :].rearrange("p a (k f) -> p (a k) f", k=2)[:, :, t * P:(t + 1) * P],
                                   ps[2 * t + b][:, :].rearrange("p (k f) -> p k f", k=4)).then_inc(h2T_ready, 1)

            def copy_score(h, t0, t1, bank, nth):
                act.wait_ge(score_mm, nth)
                for c in range(2):
                    nc.scalar.copy(scores[:, t0 * HEADS + h:(t1 - 1) * HEADS + h + 1:HEADS, c * NKEYS:(c + 1) * NKEYS],
                                   ps[bank + c][:, 0:(t1 - t0) * NKEYS].rearrange("p (t n) -> p t n", t=t1 - t0)
                                   ).then_inc(score_ready, 1)

            copy_h2T(0)
            act.wait_ge(h2_ready, NT)
            for h in range(HEADS + 1):
                if h < HEADS:
                    act.wait_ge(q_mm, h + 1)
                    nc.scalar.copy(qT[:, h % 2, 0:P], ps[h % 2][:, 0:P]).then_inc(q_copied, 1)
                if h:
                    copy_score(h - 1, 0, 1, 2 + 2 * ((h - 1) % 2), h)
            act.drain()
            nc.scalar.copy(cur.rearrange("p c n -> p (c n)"), scores[:, 0, :]).then_inc(cur_ready, 1)
            act.wait_ge(best_ready, 1)
            nc.scalar.activation(best[:, :], best[:, :], ACT.Exp, accum_out=esum[:, :]).then_inc(exp_ready, 1)
            for t in range(1, NT):
                copy_h2T(t)
            for h in range(HEADS + 1):
                if h < HEADS:
                    act.wait_ge(q_mm, HEADS + h + 1)
                    nc.scalar.copy(qT[:, h % 2, P:T], ps[2 + h % 2][:, 0:T - P]).then_inc(q_copied, 1)
                if h:
                    copy_score(h - 1, 1, NT, 4 + 2 * ((h - 1) % 2), HEADS + h)

            act.drain()
            act.wait_ge(vconsts, 2)
            with act.Fori(0, NT, 1) as t:
                with act.Fori(0, HEADS // 2, 1) as i:
                    for e in range(2):
                        step = t * HEADS + i * 2 + e
                        act.wait_ge(idx_ready, step + 1)
                        nc.scalar.copy(cur.rearrange("p c n -> p (c n)"), scores[:, step + 1, :]).then_inc(cur_ready, 1)
                        for b in range(TOPK // BATCH):
                            act.wait_ge(dots_done, step * TOPK + BATCH * (b + 1))
                            nc.scalar.activation(acts[:, e, BATCH * b:BATCH * (b + 1)],
                                                 dots[:, e, BATCH * b:BATCH * (b + 1)], ACT.Gelu).then_inc(gelu_done, 1)
                            if b == 3:
                                act.wait_ge(best_ready, step + 2)
                                nc.scalar.activation(best[:, :], best[:, :], ACT.Exp,
                                                     accum_out=esum[:, :]).then_inc(exp_ready, 1)
                root(14, 3 * NT + 1 + t)

        @block.vector
        def _(dve):
            tt, ts, stt = nc.vector.tensor_tensor, nc.vector.tensor_scalar, nc.vector.scalar_tensor_tensor

            for b in (upad[:, :, 0:PAD], wa[:, 0:PAD], wb[:, 0:PAD]):
                nc.vector.memset(b, 0.0)
            nc.vector.memset(stats[:, 15:16], EPS)
            nc.vector.memset(headmean[:, :], 0.0)
            dve.drain()
            for e in range(2):
                r = slice(64 * e, 64 * e + 64)
                nc.vector.memset(headmean[r, r], 1.0 / 64)
            dve.drain()
            dve.sem_inc(vconsts, 1)
            dve.wait_ge(consts, 5)
            nc.vector.reciprocal(invcnt[:, :], invcnt[:, :])
            dve.wait_ge(par_in, 16)
            lam = pars[:, C_LAM:C_LAM + NJ]
            ts(lscr[:, 1, :], lam, -1.0, None, ALU.mult)
            dve.drain()
            tt(lscr[:, 0, :], lam, lscr[:, 1, :], ALU.max).then_inc(lam_one, 1)
            dve.drain()
            ts(lscr[:, 1, :], lscr[:, 1, :], 0.0, None, ALU.max)
            dve.wait_ge(lam_exp, 1)
            ts(lscr[:, 0, :], lscr[:, 0, :], 1.0, None, ALU.add).then_inc(lam_one, 1)
            dve.wait_ge(lam_ln, 1)
            tt(lrate[:, :], lscr[:, 0, :], lscr[:, 1, :], ALU.add)
            dve.drain()
            ts(lrate[:, :], lrate[:, :], -4.0, None, ALU.mult).then_inc(lrate_ready, 1)
            dve.wait_ge(cact_ready, 1)
            dve.wait_ge(bada_in, 96)

            def ada_block(b):
                dve.wait_ge(ada_arr[b % ADA_RING], 16 * (b // ADA_RING + 1))
                if b >= 2:
                    dve.wait_ge(acc_mm, b - 1)
                dst = adaacc[:, b % 2, :]
                for k in range(KD):
                    w = adaring[:, b % ADA_RING, k, :]
                    if k == 0:
                        last = ts(dst, w, cact[:, 0:1], None, ALU.mult)
                    else:
                        dve.drain()
                        last = stt(dst, w, cact[:, k:k + 1], dst, ALU.mult, ALU.add)
                last.then_inc(acc_ready, 1)
                dve.wait_ge(acc_ready, b + 1)
                dve.sem_inc(ada_used, 1)

            def ada_add(b):
                dve.wait_ge(acc_mm, b + 1)
                q, c = b // 4, (b % 4) * ADA_W
                i = b % ADA_PER_G
                bank = ps[GC + i if i < GC else GC + i - 2]
                dst = ada[:, q, c:c + ADA_W]
                last = tt(dst, bank[:, 0:ADA_W], dst, ALU.add)
                if q in (1, 4):
                    dve.wait_ge(ntmp_in, 16 if q == 1 else 32)
                    dve.drain()
                    last = stt(dst, dst, 1.0, ntmp[:, c:c + ADA_W], ALU.add, ALU.mult)
                last.then_inc(ada_added, 1)

            def window(g, s):
                w = WINDOWS[g]
                dve.wait_ge(u_ready, GC * g + s + 1)
                src, shift = upad[:, s, :], 1
                for i in range(g + 1):
                    dst = wa if i % 2 == 0 else wb
                    tt(dst[:, PAD:], src[:, PAD:], src[:, PAD - shift:PAD + T - shift], ALU.add)
                    dve.drain()
                    src, shift = dst, 2 * shift
                other = wb if g % 2 == 0 else wa
                if g and s == 0:
                    dve.wait_ge(grp_mm, GC * g)
                stt(pooled[:, s, :], src[:, PAD:], 1.0 / w, upad[:, s, PAD:], ALU.mult, ALU.subtract)
                tt(other[:, PAD:PAD + w - 1], src[:, PAD:PAD + w - 1], invcnt[:, 0:w - 1], ALU.mult)
                dve.drain()
                tt(pooled[:, s, 0:w - 1], other[:, PAD:PAD + w - 1], upad[:, s, PAD:PAD + w - 1],
                   ALU.subtract).then_inc(m_ready, 1)

            for g in range(NG):
                b = ADA_PER_G * g
                ada_block(b)
                ada_block(b + 1)
                ada_add(b)
                window(g, 0)
                ada_add(b + 1)
                ada_block(b + 2)
                window(g, 1)
                ada_block(b + 3)
                ada_add(b + 2)
                window(g, 2)
                ada_block(b + 4)
                ada_add(b + 3)
                window(g, 3)
                ada_block(b + 5)
                ada_add(b + 4)
                ada_add(b + 5)
                for d in range(GC):
                    dve.wait_ge(grp_mm, GC * g + d + 1)
                    dve.wait_ge(z_ready, GC * (g + 1) + d + 1)
                    c = GC * g + d
                    stt(yin[:, c, :], ps[d][:, :], pars[:, C_SCALE + c:C_SCALE + c + 1], zs[:, d, :],
                        ALU.mult, ALU.mult).then_inc(yin_ready, 1)

            def rms_scale(src, junk, col, nth):
                dve.drain()
                nc.vector.tensor_tensor_reduce(out=junk, in0=src, in1=src, scale=1.0, scalar=0.0,
                                               op0=ALU.mult, op1=ALU.add, accum_out=stats[:, col:col + 1])
                dve.drain()
                ts(stats[:, col:col + 1], stats[:, col:col + 1], 1.0 / DM, EPS, ALU.mult, ALU.add).then_inc(var_ready, 1)
                dve.wait_ge(root_ready, nth)
                nc.vector.reciprocal(stats[:, col:col + 1], stats[:, col:col + 1])
                dve.drain()

            dve.wait_ge(x_in, 16 * NT)
            dve.wait_ge(ln_in, 32)
            for t in range(NT):
                dve.wait_ge(yout_mm, NT + t + 1)
                row, h1 = xres[:, t, :], h1tmp[:, t % 2, :]
                for half in range(2):
                    c = slice(half * T, (half + 1) * T)
                    stt(row[:, c], row[:, c], ALPHA, ps[4 * half + t][:, :], ALU.mult, ALU.add)
                    dve.drain()
                    nc.vector.bn_stats(stats[:, 6 * half:6 * half + 6], row[:, c])
                dve.drain()
                nc.vector.bn_aggr(stats[:, 12:14], stats[:, 0:12].rearrange("p (a b) -> p a b", a=2))
                dve.drain()
                ts(stats[:, 13:14], stats[:, 13:14], LN_EPS, None, ALU.add).then_inc(var_ready, 1)
                dve.wait_ge(root_ready, 2 * t + 1)
                nc.vector.reciprocal(stats[:, 13:14], stats[:, 13:14])
                dve.drain()
                ts(row, row, stats[:, 12:13], stats[:, 13:14], ALU.subtract, ALU.mult)
                dve.drain()
                tt(row, row, lnw[:, 0, :], ALU.mult)
                dve.drain()
                tt(row, row, lnw[:, 1, :], ALU.add)
                if t >= 2:
                    dve.wait_ge(h1_tr, t - 1)
                rms_scale(row, h1, 14, 2 * t + 2)
                stt(h1, row, stats[:, 14:15], ada[:, 1, :], ALU.mult, ALU.mult)
                dve.drain()
                tt(h1, h1, ada[:, 0, :], ALU.add).then_inc(h1_ready, 1)

            nc.vector.memset(xrp[:, 0:3], 0.0)
            nc.vector.memset(vp[:, 0:2], 0.0)
            dve.drain()
            dve.sem_inc(pads2, 1)

            def par(col, j):
                return pars[:, col + j:col + j + 1]

            def head_norm(n):
                j = n // 2
                y, gn, k = (gg, C_GNB, NJ + j) if n % 2 == 0 else (ya, C_GNA, j)
                dve.wait_ge(rn_ready, n + 1)
                nc.vector.reciprocal(rn[:, 0:T], rn[:, 0:T])
                dve.drain()
                stt(yT[:, k, :], y[:, 0:T], par(gn, j), rn[:, 0:T], ALU.mult, ALU.mult).then_inc(yT_ready, 1)

            for j in range(NJ):
                dve.wait_ge(xr_copied, j + 1)
                w = C_CONVB + 4 * j
                c = cx[:, 0:T]
                ts(c, xrp[:, 0:T], pars[:, w:w + 1], par(C_CBB, j), ALU.mult, ALU.add)
                for k in range(1, 4):
                    dve.drain()
                    last = stt(c, xrp[:, k:k + T], pars[:, w + k:w + k + 1], c, ALU.mult, ALU.add)
                last.then_inc(cx_ready, 1)
                if j:
                    head_norm(2 * j - 2)
                    head_norm(2 * j - 1)
                dve.wait_ge(tanh_ready, j + 1)
                th, d, a, o = rt[:, 0:T], den[:, 0:T], aa[:, 0:T], om[:, 0:T]
                u, h, y = iu[:, 0:T], hh[:, 0:T], gg[:, 0:T]
                ts(d, th, -1.0, 1.0, ALU.mult, ALU.add)
                tt(u, u, c, ALU.mult)
                dve.drain()
                nc.vector.reciprocal(d, d)
                dve.drain()
                stt(a, th, 1.0, d, ALU.add, ALU.mult)
                stt(o, th, -2.0, d, ALU.mult, ALU.mult)
                dve.drain()
                stt(o, a, 1.0, o, ALU.add, ALU.mult)
                dve.drain()
                ts(o, o, 0.0, None, ALU.max).then_inc(om_ready, 1)
                dve.wait_ge(in2_mm, 5 * j + XA + 1)
                dve.wait_ge(gc_copied, j + 1)
                tt(vp[:, 2:2 + T], gcs[:, 0:T], ps[XA][:, :], ALU.mult).then_inc(v_ready, 1)
                dve.drain()
                w = C_CONVA + 3 * j
                ca = ya[:, 0:T]
                ts(ca, vp[:, 0:T], pars[:, w:w + 1], None, ALU.mult)
                for k in range(1, 3):
                    dve.drain()
                    stt(ca, vp[:, k:k + T], pars[:, w + k:w + k + 1], ca, ALU.mult, ALU.add)
                dve.wait_ge(om_root, j + 1)
                tt(u, u, o, ALU.mult)
                dve.drain()
                nc.vector.tensor_tensor_scan(h, a, u, 0.0, ALU.mult, ALU.add)
                dve.drain()
                dve.wait_ge(gg_ready, j + 1)
                tt(y, y, h, ALU.mult).then_inc(yb_ready, 1)
                dve.wait_ge(in2_mm, 5 * j + GB + 1)
                tt(ca, ca, ps[GB][:, :], ALU.mult).then_inc(ya_ready, 1)
            head_norm(2 * NJ - 2)
            head_norm(2 * NJ - 1)

            for t in range(NT):
                dve.wait_ge(y2_mm, 2 * t + 2)
                row, hrow = xres[:, t, :], h2[:, t, :]
                dve.drain()
                for half in range(2):
                    c = slice(half * T, (half + 1) * T)
                    last = tt(xtmp[:, c], ps[2 * t + half][:, :], ada[:, 2, c], ALU.mult)
                last.then_inc(y2_read, 1)
                dve.drain()
                tt(row, row, xtmp, ALU.add)
                rms_scale(row, hrow, 14, 2 * NT + t + 1)
                stt(hrow, row, stats[:, 14:15], ada[:, 4, :], ALU.mult, ALU.mult)
                dve.drain()
                tt(hrow, hrow, ada[:, 3, :], ALU.add).then_inc(h2_ready, 1)

            cf = cand.rearrange("p a b -> p (a b)")

            def choose(part, to):
                dve.drain()
                if part < 2:
                    c = part
                    nc.vector.max(topv[:, c, 0:8], cur[:, c, :])
                    dve.drain()
                    nc.vector.max_index(topi[:, c, 0:8], topv[:, c, 0:8], cur[:, c, :])
                    nc.vector.match_replace(rest[:, 0:NKEYS], topv[:, c, 0:8], cur[:, c, :], LOWEST)
                    dve.drain()
                    nc.vector.max(topv[:, c, 8:16], rest[:, 0:NKEYS])
                    dve.drain()
                    nc.vector.max_index(topi[:, c, 8:16], topv[:, c, 8:16], rest[:, 0:NKEYS])
                    dve.drain()
                    ts(topf[:, c, :], topi[:, c, :], float(NKEYS) if c == 0 else 1.0, None, ALU.mult)
                if part == 2:
                    tt(cand, topv[:, 0, :].unsqueeze(2).to_broadcast([P, TOPK, TOPK]),
                       topv[:, 1:2, :].to_broadcast([P, TOPK, TOPK]), ALU.add)
                    dve.drain()
                    nc.vector.max(best[:, 0:8], cf)
                    dve.drain()
                    nc.vector.max_index(bpos[:, 0:8], best[:, 0:8], cf)
                    nc.vector.match_replace(rest, best[:, 0:8], cf, LOWEST)
                if part == 3:
                    nc.vector.max(best[:, 8:16], rest)
                    dve.drain()
                    nc.vector.max_index(bpos[:, 8:16], best[:, 8:16], rest)
                    nc.vector.tensor_copy(top1[:, :], best[:, 0:1])
                    dve.drain()
                    ts(ab[:, :, 0], bpos[:, :], 4, None, ALU.logical_shift_right)
                    ts(ab[:, :, 1], bpos[:, :], TOPK - 1, None, ALU.bitwise_and)
                    ts(best[:, :], best[:, :], top1[:, 0:1], None, ALU.subtract).then_inc(best_ready, 1)
                    dve.drain()
                    nc.vector.tensor_copy(abf[:, :, :], ab[:, :, :])
                if part == 4:
                    tt(hot, abf[:, :, :].unsqueeze(3).to_broadcast([P, TOPK, 2, TOPK]),
                       iota16[:, :].unsqueeze(1).unsqueeze(1).to_broadcast([P, TOPK, 2, TOPK]), ALU.is_equal)
                    dve.drain()
                    tt(hot, hot, topf[:, :, :].unsqueeze(1).to_broadcast([P, TOPK, 2, TOPK]), ALU.mult)
                    dve.drain()
                    nc.vector.tensor_reduce(idxf, hot.rearrange("p k c a -> p k (c a)"), AX.X, ALU.add)
                    dve.drain()
                    nc.vector.tensor_copy(idx[:, to, :], idxf).then_inc(idx_ready, 1)
                if part == 5:
                    nc.vector.reciprocal(esum[:, :], esum[:, :])
                    dve.drain()
                    ts(gate[:, to, :], best[:, :], esum[:, 0:1], None, ALU.mult)
                    dve.drain()

            dve.wait_ge(cur_ready, 1)
            for part in range(5):
                choose(part, 0)
            dve.wait_ge(exp_ready, 1)
            choose(5, 0)
            nc.vector.memset(scores[:, STEPS, :], 0.0)
            dve.wait_ge(score_ready, STEPS)
            nc.vector.memset(zeros, 0.0)
            dve.drain()
            dve.sem_inc(vconsts, 1)
            dve.sem_inc(outb_free, 1)
            dve.wait_ge(fing_in, 16)

            slots = {0: [0], 1: [1], 2: [2], 3: [3, 4], 5: [5]}
            with dve.Fori(0, NT, 1) as t:
                nc.vector.tensor_copy(h2cur, h2[:, t, :])
                dve.drain()
                with dve.Fori(0, HEADS // 2, 1) as i:
                    for e in range(2):
                        step = t * HEADS + i * 2 + e
                        for b in range(TOPK // BATCH):
                            for n in range(BATCH * b, BATCH * (b + 1)):
                                dve.wait_ge(arr[n % RING], step * (16 * TOPK // RING) + 16 * (n // RING + 1))
                                urow = ring[:, n % RING, 0:DM]
                                nc.vector.tensor_tensor_reduce(
                                    out=urow, in0=urow, in1=h2cur, scale=1.0, scalar=0.0, op0=ALU.mult,
                                    op1=ALU.add, accum_out=dots[:, e, n:n + 1]).then_inc(dots_done, 1)
                            if b == 0:
                                dve.wait_ge(cur_ready, step + 2)
                                dve.sem_inc(vec_go, 1)
                            if b == 5:
                                dve.wait_ge(exp_ready, step + 2)
                                dve.sem_inc(vec_go, 1)
                            for part in slots.get(b, ()):
                                choose(part, 1 - e)
                            dve.wait_ge(gelu_done, step * (TOPK // BATCH) + b + 1)
                            for n in range(BATCH * b, BATCH * (b + 1)):
                                ts(diag[:, n % RING, :], ident[:, :], acts[:, e, n:n + 1], gate[:, e, n:n + 1],
                                   ALU.mult, ALU.mult).then_inc(diag_ready, 1)
                dve.wait_ge(tile_mm, t + 1)
                dve.wait_ge(outb_free, t + 1)
                for half in range(2):
                    c = slice(half * T, (half + 1) * T)
                    last = tt(outb[:, c], ps[half][:, :], ada[:, 5, c], ALU.mult)
                last.then_inc(tile_read, 1)
                dve.drain()
                tt(outb, outb, xres[:, t, :], ALU.add)
                rms_scale(outb, h2cur, 14, 3 * NT + 1 + t)
                stt(outb, outb, stats[:, 14:15], fing, ALU.mult, ALU.mult).then_inc(out_ready, 1)


_OUT = (1, T, DM)


def kernel(**inputs):
    import numpy as np
    import concourse.bacc as bacc
    from concourse.bass_utils import run_bass_kernel_spmd

    a = {k: np.asarray(v) for k, v in inputs.items()}

    def channels(v):
        v = v.reshape(-1, v.shape[-1] // P, P)
        return v.transpose(2, 1, 0).reshape(P, -1)

    def k_major(w):
        return w.reshape(-1, P, w.shape[-1]).transpose(1, 0, 2).reshape(P, -1)

    w_in = a["pool_w_in"][0].reshape(KD, P, 2, NG, GC, P)
    w_in = w_in.transpose(3, 2, 4, 1, 0, 5).reshape(NG, 2 * GC, P, DM)
    w_in2 = a["w_in_2"][0].reshape(KD, P, 5, NJ, P)
    w_in2 = w_in2[:, :, [3, 4, 1, 2, 0]].transpose(3, 2, 1, 0, 4).reshape(NJ, 5, P, DM)
    w_ada = a["w_ada_2"][0].reshape(KD, P, NADA, ADA_W).transpose(2, 1, 0, 3).reshape(NADA, P, KD * ADA_W)
    arrays = {
        "x": a["x"][0],
        "xT": a["x"][0].T,
        "par": np.concatenate([
            channels(a["c_2"]), channels(a["pool_scale"]), channels(a["conv_a_w_2"][0]),
            channels(a["conv_b_w_2"][0]), channels(a["conv_b_b_2"]), channels(a["b_r_2"].reshape(1, -1)),
            channels(a["b_i_2"].reshape(1, -1)), channels(a["lru_lambda_2"].reshape(1, -1)), channels(a["gn_a_2"]),
            channels(a["gn_b_2"])], axis=1),
        "ln_g": a["ln_g"][0], "ln_b": a["ln_b"][0],
        "w_in": w_in,
        "w_grp": a["pool_w_grp"][0].reshape(NG, GC, P, T).transpose(0, 2, 1, 3).reshape(NG, P, GC * T),
        "w_out": a["pool_w_out"][0].reshape(NKP, P, 2, T).transpose(2, 1, 0, 3).reshape(2, P, NKP * T),
        "w_ada": w_ada,
        "b_ada": a["b_ada_2"][0], "norm1": a["norm1_g_2"][0],
        "w_in2": w_in2,
        "w_r": a["w_r_2"][0].reshape(NJ, 2, 64, 64).transpose(1, 2, 0, 3),
        "w_i": a["w_i_2"][0].reshape(NJ, 2, 64, 64).transpose(1, 2, 0, 3),
        "w_out2": k_major(a["w_out_2"][0]), "norm2": a["norm2_g_2"][0],
        "w_q": k_major(a["w_q_2"][0]),
        "keysT": a["sub_keys_2"][0].transpose(1, 3, 0, 2).reshape(P, HEADS * NKEYS),
        "experts": np.concatenate([a["expert_u_2"][0], a["expert_v_2"][0]], axis=1),
        "final_g": a["final_g_2"],
    }
    nc = bacc.Bacc("TRN2", target_bir_lowering=False, num_devices=1)
    feeds, args = {}, []
    for name, v in arrays.items():
        v = np.ascontiguousarray(v)
        feeds[f"in_{name}"] = v
        args.append(nc.dram_tensor(f"in_{name}", v.shape, mybir.dt.from_np(v.dtype), kind="ExternalInput").ap())
    args.append(nc.dram_tensor("out_x", (T, DM), mybir.dt.float32, kind="ExternalOutput").ap())
    mixers_and_peer(nc, *args)
    r = run_bass_kernel_spmd(nc, [feeds], core_ids=[0])
    return r.results[0]["out_x"].reshape(_OUT)
```

```python
import concourse.bass as bass
from concourse import mybir
from contextlib import ExitStack

P = 128
T = 512
NT = T // P
DM = 1024
KD = DM // P
WINDOWS = (2, 4, 8, 16)
NG = len(WINDOWS)
GC = 4
PAD = 16
NKP = NG * GC
ADA_W = 256
ADA_PER_G = 6
NADA = NG * ADA_PER_G
ADA_RING = 2
RAW = 3
NIN = NG * 8
NWO = 16
NRES = 4
MM2 = NIN + NWO - NRES
NJ = 4
XR, GR, GCT, XA, GB = range(5)
HEADS = 8
TOPK = 16
NKEYS = 128
DKH = 64
RING = 8
EARLY = 3
STEPS = NT * HEADS
BATCH = 2
LN_EPS = 1e-5
EPS = 1e-6
ALPHA = 2.0 ** 0.25
LOWEST = -3.0e38
C_C, C_SCALE = 0, 8
C_CONVA, C_CONVB = 24, 36
C_CBB, C_BR, C_BI, C_LAM, C_GNA, C_GNB, NPAR = 52, 56, 60, 64, 68, 72, 76


def mixers_and_peer(nc, x, xT, par, ln_g, ln_b, w_in, w_grp, w_out, w_ada, b_ada, norm1, w_in2,
                    w_r, w_i, w_out2, norm2, w_q, keysT, experts, final_g, out):
    f32, u32, f32r = mybir.dt.float32, mybir.dt.uint32, mybir.dt.float32r
    ALU, ACT, AX = mybir.AluOpType, mybir.ActivationFunctionType, mybir.AxisListType

    with ExitStack() as ctx:
        def sb(name, shape, dt=f32):
            return ctx.enter_context(nc.sbuf_tensor(name, shape, dt))

        def sem(name):
            return ctx.enter_context(nc.semaphore(name))

        xres = sb("xres", [P, NT, DM])
        ada = sb("ada", [P, 6, DM])
        lnw = sb("lnw", [P, 2, DM])
        ident = sb("ident", [P, P])
        ones = sb("ones", [P, P])
        headmean = sb("headmean", [P, P])
        pars = sb("pars", [P, NPAR])
        cact = sb("cact", [P, KD])
        invcnt = sb("invcnt", [P, PAD])
        stats = sb("stats", [P, 16])
        lrate = sb("lrate", [P, NJ])
        lscr = sb("lscr", [P, 2, NJ])

        KB = 256
        ARENA = (nc.sbuf_base + 31) // 32 * 32
        arena = sb("arena", [P, 156 * KB])

        def view(kb, n):
            at = int(kb * KB)
            return arena[:, at:at + n]

        def parts(name, kb, slots, n):
            t = nc.alloc_sbuf_tensor_at(name, [P, slots, 2, n], f32r, offset=ARENA + int(kb * 1024))
            return t

        xT_hl = parts("xT_hl", 0, KD, T)
        raw = view(32, RAW * DM).rearrange("p (r f) -> p r f", r=RAW)
        w_hl = parts("w_hl", 44, 2, DM)
        adaring = view(60, ADA_RING * KD * ADA_W).rearrange("p (r k f) -> p r k f", r=ADA_RING, k=KD)
        upad = view(76, GC * (PAD + T)).rearrange("p (c t) -> p c t", c=GC)
        wa = view(84.25, PAD + T)
        wb = view(86.3125, PAD + T)
        pooled = view(88.375, GC * T).rearrange("p (c t) -> p c t", c=GC)
        zs = view(96.375, GC * T).rearrange("p (c t) -> p c t", c=GC)
        wgrp = view(104.375, GC * T).rearrange("p (c d) -> p c d", c=GC)
        adaacc = view(112.375, ADA_PER_G * ADA_W).rearrange("p (a f) -> p a f", a=ADA_PER_G)
        ntmp = view(118.375, DM)
        xT_s = view(124, KD * T).rearrange("p (k t) -> p k t", k=KD)
        yin = view(124, NKP * T).rearrange("p (c t) -> p c t", c=NKP)
        yin_hi = nc.alloc_sbuf_tensor_at("yin_hi", [P, NKP, T], f32r, offset=ARENA)
        yin_lo = nc.alloc_sbuf_tensor_at("yin_lo", [P, NKP, T], f32r, offset=ARENA + 124 * 1024)
        wres_hl = parts("wres_hl", 60, NRES, DM)
        h1tmp = view(96.375, 2 * DM).rearrange("p (a f) -> p a f", a=2)
        h1T_hl = parts("h1T_hl", 0, KD, T)
        wout2 = view(60, KD * DM).rearrange("p (k f) -> p k f", k=KD)
        yT = view(92, 2 * NJ * T).rearrange("p (k t) -> p k t", k=2 * NJ)
        tmp = [view(108 + 2.015625 * i, T + 4) for i in range(15)]
        xrp, cx, rt, iu, den, aa, om, hh, gg, gcs, vp, ya, sqa, sqb, rn = tmp
        bdr = view(140, NJ * P).rearrange("p (j f) -> p j f", j=NJ)
        bdi = view(142, NJ * P).rearrange("p (j f) -> p j f", j=NJ)
        xtmp = view(128, DM)
        wq = view(0, KD * DM).rearrange("p (k f) -> p k f", k=KD)
        ring = view(32, RING * 2 * DM).rearrange("p (r f) -> p r f", r=RING)
        outb = view(96, DM)
        diag = view(100, RING * P).rearrange("p (r f) -> p r f", r=RING)
        h2 = view(108, (NT + 1) * DM).rearrange("p (t f) -> p t f", t=NT + 1)
        cur = view(132, 2 * NKEYS).rearrange("p (c n) -> p c n", c=2)
        cand = view(133, TOPK * TOPK).rearrange("p (a b) -> p a b", a=TOPK)
        hot = view(134, TOPK * 2 * TOPK).rearrange("p (k c a) -> p k c a", k=TOPK, c=2)
        rest = view(136, 2 * NKEYS)
        gate, dots, acts = (view(137 + 0.125 * i, 2 * TOPK).rearrange("p (e n) -> p e n", e=2) for i in range(3))
        idxf = view(137.5, TOPK)
        zeros = view(138, P)
        keys = view(144, HEADS * NKEYS).rearrange("p (h n) -> p h n", h=HEADS)
        scores = view(148, 2 * 2 * NKEYS).rearrange("p (s n) -> p s n", s=2)
        h2T = lnw[:, 0, :].rearrange("p (k f) -> p k f", k=KD)
        qT = ada[:, 0, 0:2 * P].rearrange("p (a t) -> p a t", a=2)
        h2next = ada[:, 1, :]
        h2cur = ada[:, 2, :]
        fing = ada[:, 3, :]

        def hl_of(n):
            if NIN + NWO - NRES <= n < NIN + NWO:
                return wres_hl[:, n - (NIN + NWO - NRES), :, :]
            return w_hl[:, n % 2, :, :]

        def ada_sum(i):
            return ps[GC + i % GC][:, i // GC * ADA_W:(i // GC + 1) * ADA_W]

        topv = sb("topv", [P, 2, TOPK])
        topi = sb("topi", [P, 2, TOPK], u32)
        topf = sb("topf", [P, 2, TOPK])
        best = sb("best", [P, TOPK])
        bpos = sb("bpos", [P, TOPK], u32)
        ab = sb("ab", [P, TOPK, 2], u32)
        abf = sb("abf", [P, TOPK, 2])
        iota16 = sb("iota16", [P, TOPK])
        top1 = sb("top1", [P, 1])
        esum = sb("esum", [P, 1])
        idx = sb("idx", [P, 2, TOPK], u32)

        ps = [ctx.enter_context(nc.psum_tensor(f"ps{i}", [P, T], f32)) for i in range(8)]

        par_in, bada_in, x_in, ln_in = map(sem, ("par_in", "bada_in", "x_in", "ln_in"))
        xT_in = [sem(f"xT_in{i}") for i in range(KD // 2)]
        raw_arr = [sem(f"raw_arr{r}") for r in range(RAW)]
        hi_ready, lo_ready = sem("hi_ready"), sem("lo_ready")
        w_mm = sem("w_mm")
        x_hi, x_lo = sem("x_hi"), sem("x_lo")
        yin_hi_ready, yin_lo_ready = sem("yin_hi_ready"), sem("yin_lo_ready")
        h1_hi, h1_lo = sem("h1_hi"), sem("h1_lo")
        grp_arr, ntmp_in = sem("grp_arr"), sem("ntmp_in")
        ada_arr = [sem(f"ada_arr{r}") for r in range(ADA_RING)]
        bd_in, keys_in, wout2_in, wq_in, fing_in = map(sem, ("bd_in", "keys_in", "wout2_in", "wq_in", "fing_in"))
        consts = sem("consts")
        vconsts = sem("vconsts")
        cact_ready = sem("cact_ready")
        u_ready = sem("u_ready")
        z_ready = sem("z_ready")
        m_ready = sem("m_ready")
        grp_mm = sem("grp_mm")
        yin_ready = sem("yin_ready")
        acc_ready = [sem(f"acc_ready{r}") for r in range(2)]
        acc_mm = sem("acc_mm")
        ada_used = [sem(f"ada_used{r}") for r in range(ADA_RING)]
        ada_added = sem("ada_added")
        yout_mm = sem("yout_mm")
        h1_ready, h1_tr = sem("h1_ready"), sem("h1_tr")
        lam_exp, lam_one, lam_ln, lrate_ready = map(sem, ("lam_exp", "lam_one", "lam_ln", "lrate_ready"))
        bd_zero = sem("bd_zero")
        pads2 = sem("pads2")
        gates_mm = sem("gates_mm")
        norm_mm = sem("norm_mm")
        xr_copied, gg_ready, gc_copied, sig_ready, sq_ready = map(
            sem, ("xr_copied", "gg_ready", "gc_copied", "sig_ready", "sq_ready"))
        cx_ready, yb_ready, ya_ready, yT_ready = map(sem, ("cx_ready", "yb_ready", "ya_ready", "yT_ready"))
        v_ready = sem("v_ready")
        tanh_ready = sem("tanh_ready")
        om_ready, om_root = sem("om_ready"), sem("om_root")
        var_ready, root_ready = sem("var_ready"), sem("root_ready")
        rn_ready = sem("rn_ready")
        h2n_ready = sem("h2n_ready")
        y2_mm, y2_read, h2_ready, h2_tr, h2T_ready = map(
            sem, ("y2_mm", "y2_read", "h2_ready", "h2_tr", "h2T_ready"))
        q_mm, q_copied, score_mm, score_ready = map(sem, ("q_mm", "q_copied", "score_mm", "score_ready"))
        arr = [sem(f"arr{r}") for r in range(RING)]
        slot_free = sem("slot_free")
        pool_go = sem("pool_go")
        vec_go = sem("vec_go")
        cur_ready, best_ready, exp_ready, idx_ready = map(sem, ("cur_ready", "best_ready", "exp_ready", "idx_ready"))
        dots_done, gelu_done, diag_ready = map(sem, ("dots_done", "gelu_done", "diag_ready"))
        tile_mm, tile_read = sem("tile_mm"), sem("tile_read")
        out_ready, out_stored, outb_free = sem("out_ready"), sem("out_stored"), sem("outb_free")

        block = ctx.enter_context(nc.Block())

        def row_on_all(row):
            return row.rearrange("(a n) -> a n", a=1).to_broadcast([P, DM])

        @block.sync
        def _(sp):
            def load_chunk(n):
                if n >= RAW:
                    sp.wait_ge(lo_ready, n - RAW + 1)
                if n < NIN:
                    src = w_in[n // 8, n % 8, :, :]
                elif n < NIN + NWO:
                    src = w_out[n - NIN, :, :]
                else:
                    src = w_in2[(n - NIN - NWO) // 5, (n - NIN - NWO) % 5, :, :]
                sp.dma_start(raw[:, n % RAW, :], src).then_inc(raw_arr[n % RAW], 16)

            def load_ada(b):
                if b >= ADA_RING:
                    sp.wait_ge(ada_used[b % ADA_RING], b // ADA_RING)
                sp.dma_start(adaring[:, b % ADA_RING, :, :].rearrange("p k f -> p (k f)"),
                             w_ada[b, :, :]).then_inc(ada_arr[b % ADA_RING], 16)

            def load_grp(g):
                if g:
                    sp.wait_ge(grp_mm, GC * g)
                sp.dma_start(wgrp.rearrange("p c d -> p (c d)"), w_grp[g, :, :]).then_inc(grp_arr, 16)

            for k in range(0, KD, 2):
                sp.dma_start(xT_s[:, k:k + 2, :], xT[k * P:(k + 2) * P, :].rearrange("(k p) t -> p k t", p=P)).then_inc(xT_in[k // 2], 16)
                if k == 0:
                    load_chunk(0)
                    sp.dma_start(pars[:, :], par).then_inc(par_in, 16)
            load_chunk(1)
            load_ada(0)
            load_chunk(2)
            load_ada(1)
            for g in range(NG):
                for s in range(8):
                    if 8 * g + s >= RAW:
                        load_chunk(8 * g + s)
                    if s >= 2 and ADA_PER_G * g + s - 2 >= ADA_RING:
                        load_ada(ADA_PER_G * g + s - 2)
                    if s == 5:
                        load_grp(g)
                if g == 1:
                    sp.dma_start(lnw[:, 0, :], row_on_all(ln_g)).then_inc(ln_in, 16)
                    sp.dma_start(lnw[:, 1, :], row_on_all(ln_b)).then_inc(ln_in, 16)
                if g == 2:
                    sp.wait_ge(ada_added, 2 * ADA_PER_G + ADA_PER_G)
                    sp.dma_start(ntmp, row_on_all(norm2)).then_inc(ntmp_in, 16)
                    for t in range(NT):
                        sp.dma_start(xres[:, t, :], x[t * P:(t + 1) * P, :]).then_inc(x_in, 16)
            for n in range(NIN, NIN + NWO + 2):
                load_chunk(n)
            sp.wait_ge(yout_mm, 2 * NT)
            sp.wait_ge(bd_zero, 2)
            for e in range(2):
                r = slice(64 * e, 64 * e + 64)
                sp.dma_start(bdr[r, :, r], w_r[e, :, :, :]).then_inc(bd_in, 16)
                sp.dma_start(bdi[r, :, r], w_i[e, :, :, :]).then_inc(bd_in, 16)
            sp.dma_start(keys.rearrange("p h n -> p (h n)"), keysT).then_inc(keys_in, 16)
            for n in range(NIN + NWO + 2, NIN + NWO + 5 * NJ):
                load_chunk(n)
                if n == NIN + NWO + 6:
                    sp.wait_ge(h1_tr, NT)
                    sp.dma_start(wout2.rearrange("p k f -> p (k f)"), w_out2).then_inc(wout2_in, 16)
            sp.wait_ge(w_mm, MM2 + 5 * NJ)
            sp.dma_start(wq.rearrange("p k f -> p (k f)"), w_q).then_inc(wq_in, 16)
            sp.wait_ge(h2_ready, NT)
            sp.dma_start(fing, row_on_all(final_g)).then_inc(fing_in, 16)
            with sp.Fori(0, NT, 1) as t:
                sp.wait_ge(out_ready, t + 1)
                sp.dma_start(out[bass.ds(t * P, P), :], outb).then_inc(out_stored, 16)
                sp.wait_ge(out_stored, 16 * t + 16)
                sp.sem_inc(outb_free, 1)

        @block.gpsimd
        def _(pool):
            nc.gpsimd.memset(ident[:, :], 0.0).then_inc(consts, 1)
            nc.gpsimd.memset(ones[:, :], 1.0).then_inc(consts, 1)
            nc.gpsimd.iota(iota16[:, :], pattern=[[1, TOPK]], base=0, channel_multiplier=0,
                           allow_small_or_imprecise_dtypes=True).then_inc(consts, 1)
            nc.gpsimd.iota(invcnt[:, :], pattern=[[1, PAD]], base=1, channel_multiplier=0,
                           allow_small_or_imprecise_dtypes=True).then_inc(consts, 1)
            pool.wait_ge(consts, 4)
            nc.gpsimd.affine_select(out=ident[:, :], in_=ident[:, :], compare_op=ALU.not_equal, fill=1.0,
                                    base=0, pattern=[[-1, P]], channel_multiplier=1).then_inc(consts, 1)
            def lo_part(n):
                pool.wait_ge(hi_ready, n + 1)
                nc.gpsimd.tensor_tensor(hl_of(n)[:, 1, :], raw[:, n % RAW, :], hl_of(n)[:, 0, :].bitcast(f32),
                                        ALU.subtract).then_inc(lo_ready, 1)

            def ada_quarter(b, part):
                w = adaring[:, 1, :, :]
                if part == 0:
                    pool.wait_ge(ada_arr[1], 16 * (b // ADA_RING + 1))
                if part < 2:
                    k = slice(4 * part, 4 * part + 4)
                    nc.gpsimd.tensor_tensor(w[:, k, :], w[:, k, :],
                                            cact[:, k].unsqueeze(2).to_broadcast([P, 4, ADA_W]), ALU.mult)
                if part == 2:
                    pool.drain()
                    nc.gpsimd.tensor_tensor(w[:, 0:4, :], w[:, 0:4, :], w[:, 4:8, :], ALU.add)
                if part == 3:
                    pool.drain()
                    nc.gpsimd.tensor_tensor(w[:, 0:2, :], w[:, 0:2, :], w[:, 2:4, :], ALU.add)
                    if b >= ADA_PER_G:
                        pool.wait_ge(acc_mm, b - ADA_PER_G + 1)
                    pool.drain()
                    nc.gpsimd.tensor_tensor(adaacc[:, b % ADA_PER_G, :], w[:, 0, :], w[:, 1, :],
                                            ALU.add).then_inc(acc_ready[1], 1)
                    pool.wait_ge(acc_ready[1], b // 2 + 1)
                    pool.sem_inc(ada_used[1], 1)

            for n in range(NIN + NWO + 2):
                lo_part(n)
                if n == 0:
                    pool.wait_ge(cact_ready, 1)
                if n < NIN:
                    b = ADA_PER_G * (n // 8)
                    ada_quarter(b + (1 if n % 8 < 4 else 3), n % 4)
                    if n % 8 == 7:
                        for part in range(4):
                            ada_quarter(b + 5, part)
            pool.wait_ge(yout_mm, 2 * NT)
            nc.gpsimd.memset(bdr, 0.0).then_inc(bd_zero, 1)
            nc.gpsimd.memset(bdi, 0.0).then_inc(bd_zero, 1)
            for n in range(NIN + NWO + 2, NIN + NWO + 5 * NJ):
                lo_part(n)
            pool.wait_ge(w_mm, MM2 + 5 * NJ)
            with pool.Fori(0, STEPS // 2, 1) as i:
                for e in range(2):
                    pool.wait_ge(idx_ready, 2 * i + e + 1)
                    pool.sem_inc(pool_go, 1)
                    for n in range(TOPK):
                        pool.wait_ge(slot_free, 2 * TOPK * i + TOPK * e + n + 1)
                        pool.sem_inc(pool_go, 1)
                        nc.gpsimd.indirect_dma_start(
                            ring[:, n % RING, :], None, experts,
                            bass.IndirectOffsetOnAxis(ap=idx[:, e, n:n + 1], axis=0)).then_inc(arr[n % RING], 16)

        @block.tensor
        def _(pe):
            mm = nc.tensor.matmul

            def split_mm(dst, lhs, rhs, first, final):
                mm(dst, lhsT=lhs[0], rhs=rhs[0], start=first, stop=False)
                mm(dst, lhsT=lhs[0], rhs=rhs[1], start=False, stop=False)
                return mm(dst, lhsT=lhs[1], rhs=rhs[0], start=False, stop=final)

            def chunk_mm(dst, w, x_hl):
                for k in range(KD):
                    c = slice(k * P, (k + 1) * P)
                    last = split_mm(dst, (w[:, 0, c], w[:, 1, c]), (x_hl[:, k, 0, :], x_hl[:, k, 1, :]), k == 0, k == KD - 1)
                last.then_inc(w_mm, 1)

            pe.sem_inc(yin_ready, GC)
            pe.sem_inc(z_ready, GC)
            pe.wait_ge(x_lo, KD)
            pe.wait_ge(consts, 5)
            pe.wait_ge(vconsts, 1)
            pe.sem_inc(ada_added, ADA_PER_G)
            with pe.Fori(0, NG, 1) as g:
                for s in range(2 * GC):
                    pe.wait_ge(lo_ready, 8 * g + s + 1)
                    if s < GC:
                        pe.wait_ge(yin_ready, GC * g + s + 1)
                    else:
                        pe.wait_ge(z_ready, GC * g + s - GC + 1)
                        pe.wait_ge(ada_added, ADA_PER_G * (g + 1))
                    chunk_mm(ps[s][:, :], w_hl[:, s % 2, :, :], xT_hl)
                pe.wait_ge(m_ready, GC * g + GC)
                pe.wait_ge(grp_arr, 16 * g + 16)
                for d in range(GC):
                    for c in range(GC):
                        last = mm(ps[d][:, :], lhsT=wgrp[:, c, d * P:(d + 1) * P], rhs=pooled[:, c, :],
                                  start=(c == 0), stop=(c == GC - 1))
                    last.then_inc(grp_mm, 1)
                for i in range(ADA_PER_G):
                    pe.wait_ge(acc_ready[i % 2], ADA_PER_G // 2 * g + i // 2 + 1)
                    pe.wait_ge(z_ready, GC * (g + 1) + i % GC + 1)
                    mm(ada_sum(i), lhsT=ones[:, :], rhs=adaacc[:, i, :], start=True, stop=True).then_inc(acc_mm, 1)

            pe.wait_ge(yin_ready, GC + NKP)

            def wout_mm(c, t, first, final):
                bank = ps[4 * (c // 8) + t]
                w = hl_of(NIN + c)
                for i in range(2):
                    k, f = 2 * (c % 8) + i, slice(i * T, (i + 1) * T)
                    tok = slice(t * P, (t + 1) * P)
                    last = split_mm(bank[:, :], (yin_hi[:, k, tok], yin_lo[:, k, tok]), (w[:, 0, f], w[:, 1, f]),
                                    first and i == 0, final and i == 1)
                return last

            for c in range(NWO - NRES):
                pe.wait_ge(lo_ready, NIN + c + 1)
                pe.wait_ge(yin_lo_ready, min(2 * (c % 8) + 2, NKP))
                if c == 8:
                    pe.wait_ge(ada_added, ADA_PER_G + NADA)
                for t in range(NT):
                    last = wout_mm(c, t, c % 8 == 0, c == 7)
                last.then_inc(w_mm, 1)
            pe.wait_ge(lo_ready, NIN + NWO)
            pe.wait_ge(yin_lo_ready, NKP)
            for t in range(NT):
                for c in range(NWO - NRES, NWO):
                    last = wout_mm(c, t, False, c == NWO - 1)
                last.then_inc(yout_mm, 2)
            for t in range(NT):
                pe.wait_ge(h1_ready, t + 1)
                for k in range(KD):
                    bank = ps[t] if k < 4 else ps[4 + t]
                    last = nc.tensor.transpose(bank[:, (k % 4) * P:(k % 4 + 1) * P],
                                               h1tmp[:, t % 2, k * P:(k + 1) * P], ident[:, :])
                last.then_inc(h1_tr, 1)

            def head_means(n):
                pe.wait_ge(sq_ready, n + 1)
                if n:
                    pe.wait_ge(rn_ready, n)
                mm(ps[7][:, :], lhsT=headmean[:, :], rhs=(sqb if n % 2 == 0 else sqa)[:, 0:T],
                   start=True, stop=True).then_inc(norm_mm, 1)

            pe.wait_ge(h1_lo, 2 * NT)
            read_by = {XR: xr_copied, GR: gg_ready, GCT: gc_copied, XA: v_ready, GB: ya_ready}
            for j in range(NJ):
                for s in range(5):
                    n = NIN + NWO + 5 * j + s
                    pe.wait_ge(lo_ready, n + 1)
                    if j:
                        pe.wait_ge(read_by[s], j)
                    chunk_mm(ps[s][:, :], hl_of(n), h1T_hl)
                    if j and s == XR:
                        head_means(2 * j - 2)
                    if j and s == GR:
                        head_means(2 * j - 1)
                    if s == GR:
                        pe.wait_ge(bd_in, 64)
                        pe.wait_ge(cx_ready, j + 1)
                        if j:
                            pe.wait_ge(sig_ready, 2 * j)
                        mm(ps[5][:, :], lhsT=bdr[:, j, :], rhs=cx[:, 0:T], start=True, stop=True).then_inc(gates_mm, 1)
                        mm(ps[6][:, :], lhsT=bdi[:, j, :], rhs=cx[:, 0:T], start=True, stop=True).then_inc(gates_mm, 1)

            def wout2_mm(t, half, early):
                for n, k in enumerate(k for k in range(KD) if (k % NJ < NJ - 1) == early):
                    last = mm(ps[2 * t + half][:, :], lhsT=yT[:, k, t * P:(t + 1) * P],
                              rhs=wout2[:, k, half * T:(half + 1) * T], start=early and n == 0,
                              stop=not early and n == 1)
                if not early:
                    last.then_inc(y2_mm, 1)

            pe.wait_ge(yT_ready, 2 * NJ - 2)
            pe.wait_ge(wout2_in, 16)
            wout2_mm(0, 0, True)
            head_means(2 * NJ - 2)
            head_means(2 * NJ - 1)
            pe.wait_ge(gc_copied, NJ)
            pe.wait_ge(v_ready, NJ)
            for t, half in ((0, 1), (1, 0), (1, 1)):
                wout2_mm(t, half, True)
            pe.wait_ge(yT_ready, 2 * NJ)
            for t in range(2):
                for half in range(2):
                    wout2_mm(t, half, False)

            def transpose_h2(src, bank):
                for k in range(KD):
                    last = nc.tensor.transpose(ps[bank + k // 4][:, (k % 4) * P:(k % 4 + 1) * P],
                                               src[:, k * P:(k + 1) * P], ident[:, :])
                last.then_inc(h2_tr, 1)

            def query(h, bank):
                for k in range(KD):
                    last = mm(ps[bank][:, 0:P], lhsT=wq[:, k, (h % HEADS) * P:(h % HEADS + 1) * P],
                              rhs=h2T[:, k, :], start=(k == 0), stop=(k == KD - 1))
                last.then_inc(q_mm, 1)

            def score(h, bank):
                for c in range(2):
                    r = slice(DKH * c, DKH * c + DKH)
                    last = mm(ps[bank + c][:, 0:NKEYS], lhsT=qT[r, h % 2, :], rhs=keys[r, h % HEADS, :],
                              start=True, stop=True)
                last.then_inc(score_mm, 1)

            pe.wait_ge(h2_ready, 1)
            transpose_h2(h2[:, 0, :], 0)
            pe.wait_ge(wq_in, 16)
            pe.wait_ge(keys_in, 16)
            pe.wait_ge(h2T_ready, 2)
            query(0, 4)
            pe.wait_ge(q_copied, 1)
            score(0, 6)
            pe.sem_inc(slot_free, EARLY)
            query(1, 5)
            pe.wait_ge(q_copied, 2)
            pe.wait_ge(y2_read, 2)
            score(1, 2)
            pe.wait_ge(score_ready, 2)
            for t in (2, 3):
                for half in range(2):
                    for early in (True, False):
                        wout2_mm(t, half, early)
            pe.wait_ge(y2_mm, 2 * NT)
            pe.sem_inc(slot_free, RING - EARLY)
            pe.wait_ge(y2_read, NT)

            pe.sem_inc(tile_read, 1)
            pe.wait_ge(vconsts, 2)
            zero_rows = ident[:, :].unsqueeze(1).to_broadcast([P, 4, P])
            with pe.Fori(0, NT, 1) as t:
                pe.wait_ge(tile_read, t + 1)
                for half in range(2):
                    mm(ps[half][:, :].rearrange("p (a b) -> p a b", a=4), lhsT=zeros, rhs=zero_rows, start=True, stop=False)
                for e in range(HEADS):
                    h = e + 2
                    for n in range(TOPK):
                        pe.wait_ge(diag_ready, t * (HEADS * TOPK) + TOPK * e + n + 1)
                        for half in range(2):
                            last = mm(ps[half][:, :], lhsT=diag[:, n % RING, :],
                                      rhs=ring[:, n % RING, DM + half * T:DM + (half + 1) * T],
                                      start=False, stop=False)
                        last.then_inc(slot_free, 1)
                        if n == 1:
                            if h == HEADS:
                                pe.wait_ge(h2T_ready, 2 * t + 4)
                            query(h, 2 + h % 2)
                        if n == 5:
                            pe.wait_ge(q_copied, HEADS * t + h + 1)
                            pe.wait_ge(score_ready, 2 * HEADS * t + 2 * (h - 1))
                            score(h, 4 + 2 * (h % 2))
                        if n == 7 and h == HEADS - 1:
                            pe.wait_ge(h2n_ready, t + 1)
                            transpose_h2(h2next, 2)
                for half in range(2):
                    last = mm(ps[half][:, :].rearrange("p (a b) -> p a b", a=4), lhsT=zeros, rhs=zero_rows, start=False, stop=True)
                last.then_inc(tile_mm, 1)

        @block.scalar
        def _(act):
            def hi_part(n):
                act.wait_ge(raw_arr[n % RAW], 16 * (n // RAW + 1))
                if NIN + NWO - NRES <= n < NIN + NWO:
                    for r in range(ADA_RING):
                        act.wait_ge(ada_used[r], NADA // ADA_RING)
                elif n >= 2:
                    act.wait_ge(w_mm, n - 1 - (NRES if n >= NIN + NWO else 0))
                nc.scalar.copy(hl_of(n)[:, 0, :], raw[:, n % RAW, :]).then_inc(hi_ready, 1)

            hi_part(0)
            for k in range(KD):
                act.wait_ge(xT_in[k // 2], 16)
                nc.scalar.copy(xT_hl[:, k, 0, :], xT_s[:, k, :]).then_inc(x_hi, 1)
            hi_part(1)
            for n in range(6):
                act.dma_start(ada[:, n, :], row_on_all(b_ada[n * DM:(n + 1) * DM])).then_inc(bada_in, 16)
            act.dma_start(ntmp, row_on_all(norm1)).then_inc(ntmp_in, 16)
            act.wait_ge(par_in, 16)
            nc.scalar.activation(cact[:, :], pars[:, C_C:C_C + KD], ACT.Silu).then_inc(cact_ready, 1)
            act.wait_ge(lam_one, 1)
            nc.scalar.activation(lscr[:, 0, :], lscr[:, 0, :], ACT.Exp, scale=-1.0).then_inc(lam_exp, 1)
            act.wait_ge(lam_one, 2)
            nc.scalar.activation(lscr[:, 0, :], lscr[:, 0, :], ACT.Ln).then_inc(lam_ln, 1)
            act.wait_ge(vconsts, 1)

            for g in range(NG):
                for s in range(GC):
                    act.wait_ge(w_mm, 8 * g + s + 1)
                    if g:
                        act.wait_ge(m_ready, GC * (g - 1) + s + 1)
                    nc.scalar.copy(upad[:, s, PAD:], ps[s][:, :]).then_inc(u_ready, 1)
                    hi_part(8 * g + s + 2)
                for s in range(GC):
                    act.wait_ge(w_mm, 8 * g + GC + s + 1)
                    if g:
                        act.wait_ge(yin_ready, GC * g + s + 1)
                    nc.scalar.activation(zs[:, s, :], ps[GC + s][:, :], ACT.Silu).then_inc(z_ready, 1)
                    hi_part(8 * g + GC + s + 2)
            for c in range(NKP):
                act.wait_ge(yin_ready, GC + c + 1)
                nc.scalar.copy(yin_hi[:, c, :], yin[:, c, :]).then_inc(yin_hi_ready, 1)
            for n in range(NIN + 2, NIN + NWO + 2):
                hi_part(n)

            def root(col, nth):
                act.wait_ge(var_ready, nth)
                nc.scalar.activation(stats[:, col:col + 1], stats[:, col:col + 1], ACT.Sqrt).then_inc(root_ready, 1)

            for t in range(NT + 1):
                if t < NT:
                    root(13, 2 * t + 1)
                    root(14, 2 * t + 2)
                if t:
                    act.wait_ge(h1_tr, t)
                    for b in range(2):
                        nc.scalar.copy(h1T_hl[:, 4 * b:4 * b + 4, 0, (t - 1) * P:t * P],
                                       ps[4 * b + t - 1][:, :].rearrange("p (k f) -> p k f", k=4)).then_inc(h1_hi, 1)

            act.wait_ge(lrate_ready, 1)
            act.wait_ge(pads2, 1)

            def head_root(n):
                act.wait_ge(norm_mm, n + 1)
                if n:
                    act.wait_ge(yT_ready, n)
                nc.scalar.activation(rn[:, 0:T], ps[7][:, :], ACT.Sqrt, bias=stats[:, 15:16]).then_inc(rn_ready, 1)

            def next_hi(i):
                if i + 2 < 5 * NJ:
                    hi_part(NIN + NWO + i + 2)

            for j in range(NJ):
                act.wait_ge(w_mm, MM2 + 5 * j + XR + 1)
                nc.scalar.copy(xrp[:, 3:3 + T], ps[XR][:, :]).then_inc(xr_copied, 1)
                next_hi(5 * j + XR)
                if j:
                    head_root(2 * j - 2)
                act.wait_ge(w_mm, MM2 + 5 * j + GR + 1)
                next_hi(5 * j + GR)
                if j:
                    act.wait_ge(yT_ready, 2 * j - 1)
                nc.scalar.activation(gg[:, 0:T], ps[GR][:, :], ACT.Gelu).then_inc(gg_ready, 1)
                if j:
                    head_root(2 * j - 1)
                for n, (dst, bias) in enumerate(((rt, C_BR), (iu, C_BI))):
                    act.wait_ge(gates_mm, 2 * j + n + 1)
                    nc.scalar.activation(dst[:, 0:T], ps[5 + n][:, :], ACT.Sigmoid,
                                         bias=pars[:, bias + j:bias + j + 1]).then_inc(sig_ready, 1)
                act.drain()
                nc.scalar.activation(rt[:, 0:T], rt[:, 0:T], ACT.Tanh,
                                     scale=lrate[:, j:j + 1]).then_inc(tanh_ready, 1)
                act.wait_ge(w_mm, MM2 + 5 * j + GCT + 1)
                nc.scalar.copy(gcs[:, 0:T], ps[GCT][:, :]).then_inc(gc_copied, 1)
                next_hi(5 * j + GCT)
                next_hi(5 * j + XA)
                act.wait_ge(om_ready, j + 1)
                nc.scalar.activation(om[:, 0:T], om[:, 0:T], ACT.Sqrt).then_inc(om_root, 1)
                next_hi(5 * j + GB)
                act.wait_ge(yb_ready, j + 1)
                if j:
                    act.wait_ge(norm_mm, 2 * j - 1)
                nc.scalar.activation(sqb[:, 0:T], gg[:, 0:T], ACT.Square).then_inc(sq_ready, 1)
                act.wait_ge(ya_ready, j + 1)
                if j:
                    act.wait_ge(norm_mm, 2 * j)
                nc.scalar.activation(sqa[:, 0:T], ya[:, 0:T], ACT.Square).then_inc(sq_ready, 1)

            head_root(2 * NJ - 2)
            head_root(2 * NJ - 1)
            def copy_h2T(nth, bank):
                act.wait_ge(h2_tr, nth)
                for b in range(2):
                    nc.scalar.copy(h2T[:, 4 * b:4 * b + 4, :],
                                   ps[bank + b][:, :].rearrange("p (k f) -> p k f", k=4)).then_inc(h2T_ready, 1)

            def copy_q(h, bank, nth):
                act.wait_ge(q_mm, nth)
                nc.scalar.copy(qT[:, h % 2, :], ps[bank][:, 0:P]).then_inc(q_copied, 1)

            def copy_score(dst, bank, nth):
                act.wait_ge(score_mm, nth)
                for c in range(2):
                    nc.scalar.copy(dst[:, c * NKEYS:(c + 1) * NKEYS], ps[bank + c][:, 0:NKEYS]).then_inc(score_ready, 1)

            root(14, 2 * NT + 1)
            copy_h2T(1, 0)
            root(14, 2 * NT + 2)
            copy_q(0, 4, 1)
            curf = cur.rearrange("p c n -> p (c n)")
            copy_score(curf, 6, 1)
            copy_q(1, 5, 2)
            copy_score(scores[:, 1, :], 2, 2)
            act.wait_ge(best_ready, 1)
            nc.scalar.activation(best[:, :], best[:, :], ACT.Exp, accum_out=esum[:, :]).then_inc(exp_ready, 1)
            root(14, 2 * NT + 3)
            root(14, 2 * NT + 4)

            act.wait_ge(vconsts, 2)
            with act.Fori(0, NT, 1) as t:
                for e in range(HEADS):
                    step, h = t * HEADS + e, e + 2
                    act.drain()
                    act.wait_ge(idx_ready, step + 1)
                    nc.scalar.copy(curf, scores[:, (e + 1) % 2, :]).then_inc(cur_ready, 1)
                    for b in range(TOPK // BATCH):
                        act.wait_ge(dots_done, step * TOPK + BATCH * (b + 1))
                        nc.scalar.activation(acts[:, e % 2, BATCH * b:BATCH * (b + 1)],
                                             dots[:, e % 2, BATCH * b:BATCH * (b + 1)], ACT.Gelu).then_inc(gelu_done, 1)
                        if b == 1:
                            copy_q(h, 2 + h % 2, HEADS * t + h + 1)
                        if b == 2 and h == HEADS - 2:
                            act.wait_ge(h2_tr, t + 1)
                            nc.scalar.copy(h2next, h2[:, t + 1, :]).then_inc(h2n_ready, 1)
                        if b == 3:
                            act.wait_ge(best_ready, step + 2)
                            nc.scalar.activation(best[:, :], best[:, :], ACT.Exp,
                                                 accum_out=esum[:, :]).then_inc(exp_ready, 1)
                        if b == 4:
                            copy_score(scores[:, h % 2, :], 4 + 2 * (h % 2), HEADS * t + h + 1)
                        if b == 5 and h == HEADS - 1:
                            copy_h2T(t + 2, 2)
                root(14, 3 * NT + 1 + t)

        @block.vector
        def _(dve):
            tt, ts, stt = nc.vector.tensor_tensor, nc.vector.tensor_scalar, nc.vector.scalar_tensor_tensor

            for k in range(KD):
                dve.wait_ge(x_hi, k + 1)
                tt(xT_hl[:, k, 1, :], xT_s[:, k, :], xT_hl[:, k, 0, :].bitcast(f32), ALU.subtract).then_inc(x_lo, 1)
            for b in (upad[:, :, 0:PAD], wa[:, 0:PAD], wb[:, 0:PAD]):
                nc.vector.memset(b, 0.0)
            nc.vector.memset(stats[:, 15:16], EPS)
            nc.vector.memset(headmean[:, :], 0.0)
            dve.drain()
            for e in range(2):
                r = slice(64 * e, 64 * e + 64)
                nc.vector.memset(headmean[r, r], 1.0 / 64)
            dve.drain()
            dve.sem_inc(vconsts, 1)
            dve.wait_ge(consts, 5)
            nc.vector.reciprocal(invcnt[:, :], invcnt[:, :])
            dve.wait_ge(cact_ready, 1)
            dve.wait_ge(par_in, 16)
            lam = pars[:, C_LAM:C_LAM + NJ]
            ts(lscr[:, 1, :], lam, -1.0, None, ALU.mult)
            dve.drain()
            tt(lscr[:, 0, :], lam, lscr[:, 1, :], ALU.max).then_inc(lam_one, 1)
            dve.drain()
            ts(lscr[:, 1, :], lscr[:, 1, :], 0.0, None, ALU.max)
            dve.wait_ge(lam_exp, 1)
            ts(lscr[:, 0, :], lscr[:, 0, :], 1.0, None, ALU.add).then_inc(lam_one, 1)
            dve.wait_ge(lam_ln, 1)
            tt(lrate[:, :], lscr[:, 0, :], lscr[:, 1, :], ALU.add)
            dve.drain()
            ts(lrate[:, :], lrate[:, :], -4.0, None, ALU.mult).then_inc(lrate_ready, 1)

            def ada_block(b):
                dve.wait_ge(ada_arr[0], 16 * (b // ADA_RING + 1))
                if b >= ADA_PER_G:
                    dve.wait_ge(acc_mm, b - ADA_PER_G + 1)
                dst = adaacc[:, b % ADA_PER_G, :]
                for k in range(KD):
                    w = adaring[:, 0, k, :]
                    if k == 0:
                        last = ts(dst, w, cact[:, 0:1], None, ALU.mult)
                    else:
                        dve.drain()
                        last = stt(dst, w, cact[:, k:k + 1], dst, ALU.mult, ALU.add)
                last.then_inc(acc_ready[0], 1)
                dve.wait_ge(acc_ready[0], b // 2 + 1)
                dve.sem_inc(ada_used[0], 1)

            def ada_add(b):
                dve.wait_ge(acc_mm, ADA_PER_G * (b // ADA_PER_G + 1))
                q, c = b // 4, (b % 4) * ADA_W
                dst = ada[:, q, c:c + ADA_W]
                dve.wait_ge(bada_in, 96)
                last = tt(dst, ada_sum(b % ADA_PER_G), dst, ALU.add)
                if q in (1, 4):
                    dve.wait_ge(ntmp_in, 16 if q == 1 else 32)
                    dve.drain()
                    last = stt(dst, dst, 1.0, ntmp[:, c:c + ADA_W], ALU.add, ALU.mult)
                last.then_inc(ada_added, 1)

            def window(g, s):
                w = WINDOWS[g]
                dve.wait_ge(u_ready, GC * g + s + 1)
                dve.drain()
                src, shift = upad[:, s, :], 1
                for i in range(g + 1):
                    dst = wa if i % 2 == 0 else wb
                    tt(dst[:, PAD:], src[:, PAD:], src[:, PAD - shift:PAD + T - shift], ALU.add)
                    dve.drain()
                    src, shift = dst, 2 * shift
                other = wb if g % 2 == 0 else wa
                if g and s == 0:
                    dve.wait_ge(grp_mm, GC * g)
                stt(pooled[:, s, :], src[:, PAD:], 1.0 / w, upad[:, s, PAD:], ALU.mult, ALU.subtract)
                tt(other[:, PAD:PAD + w - 1], src[:, PAD:PAD + w - 1], invcnt[:, 0:w - 1], ALU.mult)
                dve.drain()
                tt(pooled[:, s, 0:w - 1], other[:, PAD:PAD + w - 1], upad[:, s, PAD:PAD + w - 1],
                   ALU.subtract).then_inc(m_ready, 1)

            for g in range(NG):
                for s in range(GC):
                    if s % 2 == 0:
                        ada_block(ADA_PER_G * g + s)
                    window(g, s)
                ada_block(ADA_PER_G * g + GC)
                for d in range(GC):
                    dve.wait_ge(grp_mm, GC * g + d + 1)
                    dve.wait_ge(z_ready, GC * (g + 1) + d + 1)
                    c = GC * g + d
                    stt(yin[:, c, :], ps[d][:, :], pars[:, C_SCALE + c:C_SCALE + c + 1], zs[:, d, :],
                        ALU.mult, ALU.mult).then_inc(yin_ready, 1)
                for i in range(ADA_PER_G):
                    ada_add(ADA_PER_G * g + i)

            def rms_scale(src, junk, col, nth):
                dve.drain()
                nc.vector.tensor_tensor_reduce(out=junk, in0=src, in1=src, scale=1.0, scalar=0.0,
                                               op0=ALU.mult, op1=ALU.add, accum_out=stats[:, col:col + 1])
                dve.drain()
                ts(stats[:, col:col + 1], stats[:, col:col + 1], 1.0 / DM, EPS, ALU.mult, ALU.add).then_inc(var_ready, 1)
                dve.wait_ge(root_ready, nth)
                nc.vector.reciprocal(stats[:, col:col + 1], stats[:, col:col + 1])
                dve.drain()

            for c in range(NKP):
                dve.wait_ge(yin_hi_ready, c + 1)
                tt(yin_lo[:, c, :], yin[:, c, :], yin_hi[:, c, :].bitcast(f32), ALU.subtract).then_inc(yin_lo_ready, 1)

            def h1_lo_part(t):
                dve.wait_ge(h1_hi, 2 * t + 2)
                for b in range(2):
                    dst = h1T_hl[:, 4 * b:4 * b + 4, :, t * P:(t + 1) * P]
                    tt(dst[:, :, 1, :], ps[4 * b + t][:, :].rearrange("p (k f) -> p k f", k=4),
                       dst[:, :, 0, :].bitcast(f32), ALU.subtract).then_inc(h1_lo, 1)

            dve.wait_ge(x_in, 16 * NT)
            dve.wait_ge(ln_in, 32)
            for t in range(NT):
                dve.wait_ge(yout_mm, 2 * (t + 1))
                row, h1 = xres[:, t, :], h1tmp[:, t % 2, :]
                for half in range(2):
                    c = slice(half * T, (half + 1) * T)
                    stt(row[:, c], row[:, c], ALPHA, ps[4 * half + t][:, :], ALU.mult, ALU.add)
                    dve.drain()
                    nc.vector.bn_stats(stats[:, 6 * half:6 * half + 6], row[:, c])
                dve.drain()
                nc.vector.bn_aggr(stats[:, 12:14], stats[:, 0:12].rearrange("p (a b) -> p a b", a=2))
                dve.drain()
                ts(stats[:, 13:14], stats[:, 13:14], LN_EPS, None, ALU.add).then_inc(var_ready, 1)
                dve.wait_ge(root_ready, 2 * t + 1)
                nc.vector.reciprocal(stats[:, 13:14], stats[:, 13:14])
                dve.drain()
                ts(row, row, stats[:, 12:13], stats[:, 13:14], ALU.subtract, ALU.mult)
                dve.drain()
                tt(row, row, lnw[:, 0, :], ALU.mult)
                dve.drain()
                tt(row, row, lnw[:, 1, :], ALU.add)
                if t >= 2:
                    dve.wait_ge(h1_tr, t - 1)
                rms_scale(row, h1, 14, 2 * t + 2)
                stt(h1, row, stats[:, 14:15], ada[:, 1, :], ALU.mult, ALU.mult)
                dve.drain()
                tt(h1, h1, ada[:, 0, :], ALU.add).then_inc(h1_ready, 1)

            for t in range(NT):
                h1_lo_part(t)

            nc.vector.memset(xrp[:, 0:3], 0.0)
            nc.vector.memset(vp[:, 0:2], 0.0)
            dve.drain()
            dve.sem_inc(pads2, 1)

            def par(col, j):
                return pars[:, col + j:col + j + 1]

            def head_norm(n):
                j = n // 2
                y, gn, k = (gg, C_GNB, NJ + j) if n % 2 == 0 else (ya, C_GNA, j)
                dve.wait_ge(rn_ready, n + 1)
                nc.vector.reciprocal(rn[:, 0:T], rn[:, 0:T])
                dve.drain()
                stt(yT[:, k, :], y[:, 0:T], par(gn, j), rn[:, 0:T], ALU.mult, ALU.mult).then_inc(yT_ready, 1)

            for j in range(NJ):
                dve.wait_ge(xr_copied, j + 1)
                w = C_CONVB + 4 * j
                c = cx[:, 0:T]
                ts(c, xrp[:, 0:T], pars[:, w:w + 1], par(C_CBB, j), ALU.mult, ALU.add)
                for k in range(1, 4):
                    dve.drain()
                    last = stt(c, xrp[:, k:k + T], pars[:, w + k:w + k + 1], c, ALU.mult, ALU.add)
                last.then_inc(cx_ready, 1)
                if j:
                    head_norm(2 * j - 2)
                    head_norm(2 * j - 1)
                dve.wait_ge(tanh_ready, j + 1)
                th, d, a, o = rt[:, 0:T], den[:, 0:T], aa[:, 0:T], om[:, 0:T]
                u, h, y = iu[:, 0:T], hh[:, 0:T], gg[:, 0:T]
                ts(d, th, -1.0, 1.0, ALU.mult, ALU.add)
                tt(u, u, c, ALU.mult)
                dve.drain()
                nc.vector.reciprocal(d, d)
                dve.drain()
                stt(a, th, 1.0, d, ALU.add, ALU.mult)
                stt(o, th, -2.0, d, ALU.mult, ALU.mult)
                dve.drain()
                stt(o, a, 1.0, o, ALU.add, ALU.mult)
                dve.drain()
                ts(o, o, 0.0, None, ALU.max).then_inc(om_ready, 1)
                dve.wait_ge(w_mm, MM2 + 5 * j + XA + 1)
                dve.wait_ge(gc_copied, j + 1)
                tt(vp[:, 2:2 + T], gcs[:, 0:T], ps[XA][:, :], ALU.mult).then_inc(v_ready, 1)
                dve.drain()
                w = C_CONVA + 3 * j
                ca = ya[:, 0:T]
                ts(ca, vp[:, 0:T], pars[:, w:w + 1], None, ALU.mult)
                for k in range(1, 3):
                    dve.drain()
                    stt(ca, vp[:, k:k + T], pars[:, w + k:w + k + 1], ca, ALU.mult, ALU.add)
                dve.wait_ge(om_root, j + 1)
                tt(u, u, o, ALU.mult)
                dve.drain()
                nc.vector.tensor_tensor_scan(h, a, u, 0.0, ALU.mult, ALU.add)
                dve.drain()
                dve.wait_ge(gg_ready, j + 1)
                tt(y, y, h, ALU.mult).then_inc(yb_ready, 1)
                dve.wait_ge(w_mm, MM2 + 5 * j + GB + 1)
                tt(ca, ca, ps[GB][:, :], ALU.mult).then_inc(ya_ready, 1)
            head_norm(2 * NJ - 2)
            head_norm(2 * NJ - 1)

            def make_h2(t):
                dve.wait_ge(y2_mm, 2 * t + 2)
                row, hrow = xres[:, t, :], h2[:, t, :]
                dve.drain()
                for half in range(2):
                    c = slice(half * T, (half + 1) * T)
                    last = tt(xtmp[:, c], ps[2 * t + half][:, :], ada[:, 2, c], ALU.mult)
                last.then_inc(y2_read, 1)
                dve.drain()
                tt(row, row, xtmp, ALU.add)
                rms_scale(row, hrow, 14, 2 * NT + t + 1)
                stt(hrow, row, stats[:, 14:15], ada[:, 4, :], ALU.mult, ALU.mult)
                dve.drain()
                tt(hrow, hrow, ada[:, 3, :], ALU.add).then_inc(h2_ready, 1)

            make_h2(0)
            make_h2(1)

            cf = cand.rearrange("p a b -> p (a b)")

            def choose(part, to):
                dve.drain()
                if part < 2:
                    c = part
                    nc.vector.max(topv[:, c, 0:8], cur[:, c, :])
                    dve.drain()
                    nc.vector.max_index(topi[:, c, 0:8], topv[:, c, 0:8], cur[:, c, :])
                    nc.vector.match_replace(rest[:, 0:NKEYS], topv[:, c, 0:8], cur[:, c, :], LOWEST)
                    dve.drain()
                    nc.vector.max(topv[:, c, 8:16], rest[:, 0:NKEYS])
                    dve.drain()
                    nc.vector.max_index(topi[:, c, 8:16], topv[:, c, 8:16], rest[:, 0:NKEYS])
                    dve.drain()
                    ts(topf[:, c, :], topi[:, c, :], float(NKEYS) if c == 0 else 1.0, None, ALU.mult)
                if part == 2:
                    tt(cand, topv[:, 0, :].unsqueeze(2).to_broadcast([P, TOPK, TOPK]),
                       topv[:, 1:2, :].to_broadcast([P, TOPK, TOPK]), ALU.add)
                    dve.drain()
                    nc.vector.max(best[:, 0:8], cf)
                    dve.drain()
                    nc.vector.max_index(bpos[:, 0:8], best[:, 0:8], cf)
                    nc.vector.match_replace(rest, best[:, 0:8], cf, LOWEST)
                if part == 3:
                    nc.vector.max(best[:, 8:16], rest)
                    dve.drain()
                    nc.vector.max_index(bpos[:, 8:16], best[:, 8:16], rest)
                    nc.vector.tensor_copy(top1[:, :], best[:, 0:1])
                    dve.drain()
                    ts(ab[:, :, 0], bpos[:, :], 4, None, ALU.logical_shift_right)
                    ts(ab[:, :, 1], bpos[:, :], TOPK - 1, None, ALU.bitwise_and)
                    ts(best[:, :], best[:, :], top1[:, 0:1], None, ALU.subtract).then_inc(best_ready, 1)
                    dve.drain()
                    nc.vector.tensor_copy(abf[:, :, :], ab[:, :, :])
                if part == 4:
                    tt(hot, abf[:, :, :].unsqueeze(3).to_broadcast([P, TOPK, 2, TOPK]),
                       iota16[:, :].unsqueeze(1).unsqueeze(1).to_broadcast([P, TOPK, 2, TOPK]), ALU.is_equal)
                    dve.drain()
                    tt(hot, hot, topf[:, :, :].unsqueeze(1).to_broadcast([P, TOPK, 2, TOPK]), ALU.mult)
                    dve.drain()
                    nc.vector.tensor_reduce(idxf, hot.rearrange("p k c a -> p k (c a)"), AX.X, ALU.add)
                    dve.drain()
                    nc.vector.tensor_copy(idx[:, to, :], idxf).then_inc(idx_ready, 1)
                if part == 5:
                    nc.vector.reciprocal(esum[:, :], esum[:, :])
                    dve.drain()
                    ts(gate[:, to, :], best[:, :], esum[:, 0:1], None, ALU.mult)
                    dve.drain()

            dve.wait_ge(score_ready, 2)
            for part in range(5):
                choose(part, 0)
            dve.wait_ge(exp_ready, 1)
            choose(5, 0)
            make_h2(2)
            make_h2(3)
            nc.vector.memset(h2[:, NT, :], 0.0)
            nc.vector.memset(zeros, 0.0)
            dve.drain()
            dve.sem_inc(vconsts, 1)
            dve.sem_inc(outb_free, 1)
            dve.wait_ge(fing_in, 16)

            slots = {0: [0], 1: [1], 2: [2], 3: [3, 4], 5: [5]}
            with dve.Fori(0, NT, 1) as t:
                nc.vector.tensor_copy(h2cur, h2[:, t, :])
                dve.drain()
                with dve.Fori(0, HEADS // 2, 1) as i:
                    for e in range(2):
                        step = t * HEADS + i * 2 + e
                        for b in range(TOPK // BATCH):
                            for n in range(BATCH * b, BATCH * (b + 1)):
                                dve.wait_ge(arr[n % RING], step * (16 * TOPK // RING) + 16 * (n // RING + 1))
                                urow = ring[:, n % RING, 0:DM]
                                nc.vector.tensor_tensor_reduce(
                                    out=urow, in0=urow, in1=h2cur, scale=1.0, scalar=0.0, op0=ALU.mult,
                                    op1=ALU.add, accum_out=dots[:, e, n:n + 1]).then_inc(dots_done, 1)
                            if b == 0:
                                dve.wait_ge(cur_ready, step + 1)
                                dve.sem_inc(vec_go, 1)
                            if b == 5:
                                dve.wait_ge(exp_ready, step + 2)
                                dve.sem_inc(vec_go, 1)
                            for part in slots.get(b, ()):
                                choose(part, 1 - e)
                            dve.wait_ge(gelu_done, step * (TOPK // BATCH) + b + 1)
                            for n in range(BATCH * b, BATCH * (b + 1)):
                                ts(diag[:, n % RING, :], ident[:, :], acts[:, e, n:n + 1], gate[:, e, n:n + 1],
                                   ALU.mult, ALU.mult).then_inc(diag_ready, 1)
                dve.wait_ge(tile_mm, t + 1)
                dve.wait_ge(outb_free, t + 1)
                for half in range(2):
                    c = slice(half * T, (half + 1) * T)
                    last = tt(outb[:, c], ps[half][:, :], ada[:, 5, c], ALU.mult)
                last.then_inc(tile_read, 1)
                dve.drain()
                tt(outb, outb, xres[:, t, :], ALU.add)
                rms_scale(outb, h2cur, 14, 3 * NT + 1 + t)
                stt(outb, outb, stats[:, 14:15], fing, ALU.mult, ALU.mult).then_inc(out_ready, 1)


_OUT = (1, T, DM)


def kernel(**inputs):
    import numpy as np
    import concourse.bacc as bacc
    from concourse.bass_utils import run_bass_kernel_spmd

    a = {k: np.asarray(v) for k, v in inputs.items()}

    def channels(v):
        v = v.reshape(-1, v.shape[-1] // P, P)
        return v.transpose(2, 1, 0).reshape(P, -1)

    def k_major(w):
        return w.reshape(-1, P, w.shape[-1]).transpose(1, 0, 2).reshape(P, -1)

    w_in = a["pool_w_in"][0].reshape(KD, P, 2, NG, GC, P)
    w_in = w_in.transpose(3, 2, 4, 1, 0, 5).reshape(NG, 2 * GC, P, DM)
    w_in2 = a["w_in_2"][0].reshape(KD, P, 5, NJ, P)
    w_in2 = w_in2[:, :, [3, 4, 1, 2, 0]].transpose(3, 2, 1, 0, 4).reshape(NJ, 5, P, DM)
    w_ada = a["w_ada_2"][0].reshape(KD, P, NADA, ADA_W).transpose(2, 1, 0, 3).reshape(NADA, P, KD * ADA_W)
    arrays = {
        "x": a["x"][0],
        "xT": a["x"][0].T,
        "par": np.concatenate([
            channels(a["c_2"]), channels(a["pool_scale"]), channels(a["conv_a_w_2"][0]),
            channels(a["conv_b_w_2"][0]), channels(a["conv_b_b_2"]), channels(a["b_r_2"].reshape(1, -1)),
            channels(a["b_i_2"].reshape(1, -1)), channels(a["lru_lambda_2"].reshape(1, -1)), channels(a["gn_a_2"]),
            channels(a["gn_b_2"])], axis=1),
        "ln_g": a["ln_g"][0], "ln_b": a["ln_b"][0],
        "w_in": w_in,
        "w_grp": a["pool_w_grp"][0].reshape(NG, GC, P, T).transpose(0, 2, 1, 3).reshape(NG, P, GC * T),
        "w_out": a["pool_w_out"][0].reshape(8, 2, P, 2, T).transpose(3, 0, 2, 1, 4).reshape(NWO, P, DM),
        "w_ada": w_ada,
        "b_ada": a["b_ada_2"][0], "norm1": a["norm1_g_2"][0],
        "w_in2": w_in2,
        "w_r": a["w_r_2"][0].reshape(NJ, 2, 64, 64).transpose(1, 2, 0, 3),
        "w_i": a["w_i_2"][0].reshape(NJ, 2, 64, 64).transpose(1, 2, 0, 3),
        "w_out2": k_major(a["w_out_2"][0]), "norm2": a["norm2_g_2"][0],
        "w_q": k_major(a["w_q_2"][0]),
        "keysT": a["sub_keys_2"][0].transpose(1, 3, 0, 2).reshape(P, HEADS * NKEYS),
        "experts": np.concatenate([a["expert_u_2"][0], a["expert_v_2"][0]], axis=1),
        "final_g": a["final_g_2"],
    }
    nc = bacc.Bacc("TRN2", target_bir_lowering=False, num_devices=1)
    feeds, args = {}, []
    for name, v in arrays.items():
        v = np.ascontiguousarray(v)
        feeds[f"in_{name}"] = v
        args.append(nc.dram_tensor(f"in_{name}", v.shape, mybir.dt.from_np(v.dtype), kind="ExternalInput").ap())
    args.append(nc.dram_tensor("out_x", (T, DM), mybir.dt.float32, kind="ExternalOutput").ap())
    mixers_and_peer(nc, *args)
    r = run_bass_kernel_spmd(nc, [feeds], core_ids=[0])
    return r.results[0]["out_x"].reshape(_OUT)
```

```python
import concourse.bass as bass
from concourse import mybir
from contextlib import ExitStack

P = 128
T = 512
NT = T // P
DM = 1024
KD = DM // P
WINDOWS = (2, 4, 8, 16)
NG = len(WINDOWS)
GC = 4
PAD = 16
NKP = NG * GC
ADA_W = 256
ADA_PER_G = 6
NADA = NG * ADA_PER_G
ADA_RING = 2
RAW = 3
NIN = NG * 8
NWO = 16
NRES = 6
MM2 = NIN + NWO - NRES
NJ = 4
XR, GR, GCT, XA, GB = range(5)
HEADS = 8
TOPK = 16
NKEYS = 128
DKH = 64
RING = 8
EARLY = 3
STEPS = NT * HEADS
BATCH = 2
LN_EPS = 1e-5
EPS = 1e-6
ALPHA = 2.0 ** 0.25
LOWEST = -3.0e38
C_C, C_SCALE = 0, 8
C_CONVA, C_CONVB = 24, 36
C_CBB, C_BR, C_BI, C_LAM, C_GNA, C_GNB, NPAR = 52, 56, 60, 64, 68, 72, 76


def mixers_and_peer(nc, x, xT, par, ln_g, ln_b, w_in, w_grp, w_out, w_ada, b_ada, norm1, w_in2,
                    w_r, w_i, w_out2, norm2, w_q, keysT, experts, final_g, out):
    f32, u32, f32r = mybir.dt.float32, mybir.dt.uint32, mybir.dt.float32r
    ALU, ACT, AX = mybir.AluOpType, mybir.ActivationFunctionType, mybir.AxisListType

    with ExitStack() as ctx:
        def sb(name, shape, dt=f32):
            return ctx.enter_context(nc.sbuf_tensor(name, shape, dt))

        def sem(name):
            return ctx.enter_context(nc.semaphore(name))

        XRES = (nc.sbuf_base + 31) // 32 * 32
        xres = sb("xres", [P, NT, DM])
        ada = sb("ada", [P, 6, DM])
        lnw = sb("lnw", [P, 2, DM])
        ident = sb("ident", [P, P])
        ones = sb("ones", [P, P])
        headmean = sb("headmean", [P, P])
        pars = sb("pars", [P, NPAR])
        cact = sb("cact", [P, KD])
        invcnt = sb("invcnt", [P, PAD])
        stats = sb("stats", [P, 17])
        lrate = sb("lrate", [P, NJ])
        lscr = sb("lscr", [P, 2, NJ])

        KB = 256
        ARENA = (nc.sbuf_base + 31) // 32 * 32
        arena = sb("arena", [P, 156 * KB])

        def view(kb, n):
            at = int(kb * KB)
            return arena[:, at:at + n]

        def parts(name, kb, slots, n):
            t = nc.alloc_sbuf_tensor_at(name, [P, slots, 2, n], f32r, offset=ARENA + int(kb * 1024))
            return t

        xT_hl = parts("xT_hl", 0, KD, T)
        raw = view(32, RAW * DM).rearrange("p (r f) -> p r f", r=RAW)
        w_hl = parts("w_hl", 44, 2, DM)
        adaring = view(60, ADA_RING * KD * ADA_W).rearrange("p (r k f) -> p r k f", r=ADA_RING, k=KD)
        upad = view(76, GC * (PAD + T)).rearrange("p (c t) -> p c t", c=GC)
        wa = view(84.25, PAD + T)
        wb = view(86.3125, PAD + T)
        pooled = view(88.375, GC * T).rearrange("p (c t) -> p c t", c=GC)
        zs = view(96.375, GC * T).rearrange("p (c t) -> p c t", c=GC)
        wgrp = view(104.375, GC * T).rearrange("p (c d) -> p c d", c=GC)
        pooled_hi = nc.alloc_sbuf_tensor_at("pooled_hi", [P, GC, T], f32r, offset=XRES)
        wgrp_hi = nc.alloc_sbuf_tensor_at("wgrp_hi", [P, GC, T], f32r, offset=XRES + GC * T * 4)
        pooled_lo = nc.alloc_sbuf_tensor_at("pooled_lo", [P, GC, T], f32r, offset=ARENA + int(88.375 * 1024))
        wgrp_lo = nc.alloc_sbuf_tensor_at("wgrp_lo", [P, GC, T], f32r, offset=ARENA + int(104.375 * 1024))
        adaacc = view(112.375, ADA_PER_G * ADA_W).rearrange("p (a f) -> p a f", a=ADA_PER_G)
        ntmp = view(118.375, DM)
        xT_s = view(124, KD * T).rearrange("p (k t) -> p k t", k=KD)
        yin = view(124, NKP * T).rearrange("p (c t) -> p c t", c=NKP)
        yin_hi = nc.alloc_sbuf_tensor_at("yin_hi", [P, NKP, T], f32r, offset=ARENA)
        yin_lo = nc.alloc_sbuf_tensor_at("yin_lo", [P, NKP, T], f32r, offset=ARENA + 124 * 1024)
        wres_hl = parts("wres_hl", 60, 4, DM)
        wres2_hl = parts("wres2_hl", 104.375, NRES - 4, DM)
        junk1 = view(92.25, DM)
        h1tmp = view(96.375, 2 * DM).rearrange("p (a f) -> p a f", a=2)
        h1T_hl = parts("h1T_hl", 0, KD, T)
        h1T = view(124, KD * T).rearrange("p (k t) -> p k t", k=KD)
        wout2 = view(60, KD * DM).rearrange("p (k f) -> p k f", k=KD)
        yT = view(92, 2 * NJ * T).rearrange("p (k t) -> p k t", k=2 * NJ)
        tmp = [view(108 + 2.015625 * i, T + 4) for i in range(15)]
        xrp, cx, rt, iu, den, aa, om, hh, gg, gcs, vp, ya, sqa, sqb, rn = tmp
        bdr = view(140, NJ * P).rearrange("p (j f) -> p j f", j=NJ)
        bdi = view(142, NJ * P).rearrange("p (j f) -> p j f", j=NJ)
        xtmp = view(128, DM)
        junk2 = view(151, DM)
        wq = view(0, KD * DM).rearrange("p (k f) -> p k f", k=KD)
        ring = view(32, RING * 2 * DM).rearrange("p (r f) -> p r f", r=RING)
        outb = view(96, DM)
        diag = view(100, RING * P).rearrange("p (r f) -> p r f", r=RING)
        h2 = view(108, (NT + 1) * DM).rearrange("p (t f) -> p t f", t=NT + 1)
        cur = view(132, 2 * NKEYS).rearrange("p (c n) -> p c n", c=2)
        cand = view(133, TOPK * TOPK).rearrange("p (a b) -> p a b", a=TOPK)
        hot = view(134, TOPK * 2 * TOPK).rearrange("p (k c a) -> p k c a", k=TOPK, c=2)
        rest = view(136, 2 * NKEYS)
        gate, dots, acts = (view(137 + 0.125 * i, 2 * TOPK).rearrange("p (e n) -> p e n", e=2) for i in range(3))
        idxf = view(137.5, TOPK)
        keys = view(144, HEADS * NKEYS).rearrange("p (h n) -> p h n", h=HEADS)
        h2T = lnw[:, 0, :].rearrange("p (k f) -> p k f", k=KD)
        qT = ada[:, 0, 0:2 * P].rearrange("p (a t) -> p a t", a=2)
        h2next = ada[:, 1, :]
        h2cur = ada[:, 2, :]
        fing = ada[:, 3, :]

        def hl_of(n):
            if NIN + NWO - NRES <= n < NIN + NWO:
                i = n - (NIN + NWO - NRES)
                return wres_hl[:, i, :, :] if i < 4 else wres2_hl[:, i - 4, :, :]
            return w_hl[:, n % 2, :, :]

        def ada_sum(i):
            return ps[GC + i % GC][:, i // GC * ADA_W:(i // GC + 1) * ADA_W]

        topv = sb("topv", [P, 2, TOPK])
        topi = sb("topi", [P, 2, TOPK], u32)
        topf = sb("topf", [P, 2, TOPK])
        best = sb("best", [P, TOPK])
        bpos = sb("bpos", [P, TOPK], u32)
        ab = sb("ab", [P, TOPK, 2], u32)
        abf = sb("abf", [P, TOPK, 2])
        iota16 = sb("iota16", [P, TOPK])
        top1 = sb("top1", [P, 1])
        esum = sb("esum", [P, 1])
        idx = sb("idx", [P, 2, TOPK], u32)

        ps = [ctx.enter_context(nc.psum_tensor(f"ps{i}", [P, T], f32)) for i in range(8)]

        par_in, bada_in, x_in, ln_in = map(sem, ("par_in", "bada_in", "x_in", "ln_in"))
        xT_in = [sem(f"xT_in{i}") for i in range(KD // 2)]
        raw_arr = [sem(f"raw_arr{r}") for r in range(RAW)]
        hi_ready, lo_ready = sem("hi_ready"), sem("lo_ready")
        w_mm = sem("w_mm")
        x_hi, x_lo = sem("x_hi"), sem("x_lo")
        yin_hi_ready, yin_lo_ready = sem("yin_hi_ready"), sem("yin_lo_ready")
        h1_hi, h1_lo = sem("h1_hi"), sem("h1_lo")
        grp_arr, ntmp_in = sem("grp_arr"), sem("ntmp_in")
        ada_arr = [sem(f"ada_arr{r}") for r in range(ADA_RING)]
        bd_in, keys_in, wout2_in, wq_in, fing_in = map(sem, ("bd_in", "keys_in", "wout2_in", "wq_in", "fing_in"))
        consts = sem("consts")
        vconsts = sem("vconsts")
        cact_ready = sem("cact_ready")
        u_ready = sem("u_ready")
        z_ready = sem("z_ready")
        m_ready = sem("m_ready")
        grp_hi, grp_lo = sem("grp_hi"), sem("grp_lo")
        grp_mm = sem("grp_mm")
        yin_ready = sem("yin_ready")
        acc_ready = [sem(f"acc_ready{r}") for r in range(2)]
        acc_mm = sem("acc_mm")
        ada_used = [sem(f"ada_used{r}") for r in range(ADA_RING)]
        ada_added = sem("ada_added")
        yout_mm = sem("yout_mm")
        h1_ready, h1_tr = sem("h1_ready"), sem("h1_tr")
        lam_exp, lam_one, lam_ln, lrate_ready = map(sem, ("lam_exp", "lam_one", "lam_ln", "lrate_ready"))
        bd_zero = sem("bd_zero")
        pads2 = sem("pads2")
        gates_mm = sem("gates_mm")
        norm_mm = sem("norm_mm")
        xr_copied, gg_ready, gc_copied, sig_ready, sq_ready = map(
            sem, ("xr_copied", "gg_ready", "gc_copied", "sig_ready", "sq_ready"))
        cx_ready, yb_ready, ya_ready, yT_ready = map(sem, ("cx_ready", "yb_ready", "ya_ready", "yT_ready"))
        v_ready = sem("v_ready")
        tanh_ready = sem("tanh_ready")
        om_ready, om_root = sem("om_ready"), sem("om_root")
        var_ready, row_ready, root_ready = sem("var_ready"), sem("row_ready"), sem("root_ready")
        rn_ready = sem("rn_ready")
        h2n_ready = sem("h2n_ready")
        y2_mm, y2_read, h2_ready, h2_tr, h2T_ready = map(
            sem, ("y2_mm", "y2_read", "h2_ready", "h2_tr", "h2T_ready"))
        q_mm, q_copied, score_mm, score_ready = map(sem, ("q_mm", "q_copied", "score_mm", "score_ready"))
        arr = [sem(f"arr{r}") for r in range(RING)]
        slot_free = sem("slot_free")
        pool_go = sem("pool_go")
        vec_go = sem("vec_go")
        best_ready, exp_ready, idx_ready = map(sem, ("best_ready", "exp_ready", "idx_ready"))
        dots_done, gelu_done, diag_ready = map(sem, ("dots_done", "gelu_done", "diag_ready"))
        tile_mm, tile_read = sem("tile_mm"), sem("tile_read")
        out_ready, out_stored, outb_free = sem("out_ready"), sem("out_stored"), sem("outb_free")

        block = ctx.enter_context(nc.Block())

        def row_on_all(row):
            return row.rearrange("(a n) -> a n", a=1).to_broadcast([P, DM])

        @block.sync
        def _(sp):
            def load_chunk(n):
                if n >= RAW:
                    sp.wait_ge(lo_ready, n - RAW + 1)
                if n < NIN:
                    src = w_in[n // 8, n % 8, :, :]
                elif n < NIN + NWO:
                    src = w_out[n - NIN, :, :]
                else:
                    src = w_in2[(n - NIN - NWO) // 5, (n - NIN - NWO) % 5, :, :]
                sp.dma_start(raw[:, n % RAW, :], src).then_inc(raw_arr[n % RAW], 16)

            def load_ada(b):
                if b >= ADA_RING:
                    sp.wait_ge(ada_used[b % ADA_RING], b // ADA_RING)
                sp.dma_start(adaring[:, b % ADA_RING, :, :].rearrange("p k f -> p (k f)"),
                             w_ada[b, :, :]).then_inc(ada_arr[b % ADA_RING], 16)

            def load_grp(g):
                if g:
                    sp.wait_ge(grp_mm, GC * g)
                sp.dma_start(wgrp.rearrange("p c d -> p (c d)"), w_grp[g, :, :]).then_inc(grp_arr, 16)

            for k in range(0, KD, 2):
                sp.dma_start(xT_s[:, k:k + 2, :], xT[k * P:(k + 2) * P, :].rearrange("(k p) t -> p k t", p=P)).then_inc(xT_in[k // 2], 16)
                if k == 0:
                    load_chunk(0)
                    sp.dma_start(pars[:, :], par).then_inc(par_in, 16)
            load_chunk(1)
            load_chunk(2)
            load_ada(0)
            load_ada(1)
            for g in range(NG):
                for s in range(8):
                    if 8 * g + s >= RAW:
                        load_chunk(8 * g + s)
                    if s >= 2 and ADA_PER_G * g + s - 2 >= ADA_RING:
                        load_ada(ADA_PER_G * g + s - 2)
                    if s == 3:
                        load_grp(g)
                if g == 1:
                    sp.dma_start(lnw[:, 0, :], row_on_all(ln_g)).then_inc(ln_in, 16)
                    sp.dma_start(lnw[:, 1, :], row_on_all(ln_b)).then_inc(ln_in, 16)
                if g == 2:
                    sp.wait_ge(ada_added, 2 * ADA_PER_G + ADA_PER_G)
                    sp.dma_start(ntmp, row_on_all(norm2)).then_inc(ntmp_in, 16)
            for n in range(NIN, NIN + NWO + 2):
                load_chunk(n)
                if NIN + 4 <= n < NIN + 4 + NT:
                    t = n - NIN - 4
                    sp.wait_ge(grp_mm, NKP)
                    sp.dma_start(xres[:, t, :], x[t * P:(t + 1) * P, :]).then_inc(x_in, 16)
            sp.wait_ge(yout_mm, 2 * NT)
            sp.wait_ge(bd_zero, 2)
            for e in range(2):
                r = slice(64 * e, 64 * e + 64)
                sp.dma_start(bdr[r, :, r], w_r[e, :, :, :]).then_inc(bd_in, 16)
                sp.dma_start(bdi[r, :, r], w_i[e, :, :, :]).then_inc(bd_in, 16)
            sp.dma_start(keys.rearrange("p h n -> p (h n)"), keysT).then_inc(keys_in, 16)
            for n in range(NIN + NWO + 2, NIN + NWO + 5 * NJ):
                load_chunk(n)
                if n == NIN + NWO + 6:
                    sp.wait_ge(h1_tr, NT)
                    sp.dma_start(wout2.rearrange("p k f -> p (k f)"), w_out2).then_inc(wout2_in, 16)
            sp.wait_ge(w_mm, MM2 + 5 * NJ)
            sp.dma_start(wq.rearrange("p k f -> p (k f)"), w_q).then_inc(wq_in, 16)
            sp.wait_ge(h2_ready, NT)
            sp.dma_start(fing, row_on_all(final_g)).then_inc(fing_in, 16)
            with sp.Fori(0, NT, 1) as t:
                for half in range(2):
                    sp.wait_ge(out_ready, 2 * t + half + 1)
                    c = slice(half * T, (half + 1) * T)
                    sp.dma_start(out[bass.ds(t * P, P), c], outb[:, c]).then_inc(out_stored, 16)
                sp.wait_ge(out_stored, 32 * t + 32)
                sp.sem_inc(outb_free, 1)

        @block.gpsimd
        def _(pool):
            nc.gpsimd.memset(ident[:, :], 0.0).then_inc(consts, 1)
            nc.gpsimd.memset(ones[:, :], 1.0).then_inc(consts, 1)
            nc.gpsimd.iota(iota16[:, :], pattern=[[1, TOPK]], base=0, channel_multiplier=0,
                           allow_small_or_imprecise_dtypes=True).then_inc(consts, 1)
            nc.gpsimd.iota(invcnt[:, :], pattern=[[1, PAD]], base=1, channel_multiplier=0,
                           allow_small_or_imprecise_dtypes=True).then_inc(consts, 1)
            pool.wait_ge(consts, 4)
            nc.gpsimd.affine_select(out=ident[:, :], in_=ident[:, :], compare_op=ALU.not_equal, fill=1.0,
                                    base=0, pattern=[[-1, P]], channel_multiplier=1).then_inc(consts, 1)
            def lo_part(n):
                pool.wait_ge(hi_ready, n + 1)
                nc.gpsimd.tensor_tensor(hl_of(n)[:, 1, :], raw[:, n % RAW, :], hl_of(n)[:, 0, :].bitcast(f32),
                                        ALU.subtract).then_inc(lo_ready, 1)

            def ada_quarter(b, part):
                w = adaring[:, 1, :, :]
                if part == 0:
                    pool.wait_ge(ada_arr[1], 16 * (b // ADA_RING + 1))
                if part < 2:
                    k = slice(4 * part, 4 * part + 4)
                    nc.gpsimd.tensor_tensor(w[:, k, :], w[:, k, :],
                                            cact[:, k].unsqueeze(2).to_broadcast([P, 4, ADA_W]), ALU.mult)
                if part == 2:
                    pool.drain()
                    nc.gpsimd.tensor_tensor(w[:, 0:4, :], w[:, 0:4, :], w[:, 4:8, :], ALU.add)
                if part == 3:
                    pool.drain()
                    nc.gpsimd.tensor_tensor(w[:, 0:2, :], w[:, 0:2, :], w[:, 2:4, :], ALU.add)
                    if b >= ADA_PER_G:
                        pool.wait_ge(acc_mm, b - ADA_PER_G + 1)
                    pool.drain()
                    nc.gpsimd.tensor_tensor(adaacc[:, b % ADA_PER_G, :], w[:, 0, :], w[:, 1, :],
                                            ALU.add).then_inc(acc_ready[1], 1)
                    pool.wait_ge(acc_ready[1], 2 * (b // ADA_PER_G) + (b % ADA_PER_G) // 2 + 1)
                    pool.sem_inc(ada_used[1], 1)

            for n in range(NIN + NWO + 2):
                lo_part(n)
                if n == 0:
                    pool.wait_ge(cact_ready, 1)
                if n < NIN:
                    b = ADA_PER_G * (n // 8)
                    for part in {0: (), 1: (0, 1)}.get(n, (n % 4,)):
                        ada_quarter(b + (1 if n % 8 < 4 else 3), part)
            for t in range(NT):
                for b in range(2):
                    pool.wait_ge(h1_hi, 4 * t + 2 * b + 2)
                    k, tok = slice(4 * b, 4 * b + 4), slice(t * P, (t + 1) * P)
                    nc.gpsimd.tensor_tensor(h1T_hl[:, k, 1, tok], h1T[:, k, tok],
                                            h1T_hl[:, k, 0, tok].bitcast(f32), ALU.subtract).then_inc(h1_lo, 1)
            pool.wait_ge(yout_mm, 2 * NT)
            nc.gpsimd.memset(bdr, 0.0).then_inc(bd_zero, 1)
            nc.gpsimd.memset(bdi, 0.0).then_inc(bd_zero, 1)
            for n in range(NIN + NWO + 2, NIN + NWO + 5 * NJ):
                lo_part(n)
            pool.wait_ge(w_mm, MM2 + 5 * NJ)
            with pool.Fori(0, STEPS // 2, 1) as i:
                for e in range(2):
                    pool.wait_ge(idx_ready, 2 * i + e + 1)
                    pool.sem_inc(pool_go, 1)
                    for n in range(TOPK):
                        pool.wait_ge(slot_free, 2 * TOPK * i + TOPK * e + n + 1)
                        pool.sem_inc(pool_go, 1)
                        nc.gpsimd.indirect_dma_start(
                            ring[:, n % RING, :], None, experts,
                            bass.IndirectOffsetOnAxis(ap=idx[:, e, n:n + 1], axis=0)).then_inc(arr[n % RING], 16)

        @block.tensor
        def _(pe):
            mm = nc.tensor.matmul

            def split_mm(dst, lhs, rhs, first, final):
                mm(dst, lhsT=lhs[0], rhs=rhs[0], start=first, stop=False)
                mm(dst, lhsT=lhs[0], rhs=rhs[1], start=False, stop=False)
                return mm(dst, lhsT=lhs[1], rhs=rhs[0], start=False, stop=final)

            def chunk_mm(dst, w, x_hl, tok=slice(0, T), x_ready=None):
                for k in range(KD):
                    if x_ready is not None:
                        pe.wait_ge(x_ready, k + 1)
                    c = slice(k * P, (k + 1) * P)
                    last = split_mm(dst[:, tok], (w[:, 0, c], w[:, 1, c]), (x_hl[:, k, 0, tok], x_hl[:, k, 1, tok]),
                                    k == 0, k == KD - 1)
                if tok.stop == T:
                    last.then_inc(w_mm, 1)

            pe.sem_inc(yin_ready, GC)
            pe.sem_inc(z_ready, GC)
            pe.wait_ge(consts, 5)
            pe.wait_ge(vconsts, 1)
            pe.sem_inc(ada_added, ADA_PER_G)
            with pe.Fori(0, NG, 1) as g:
                for s in range(2 * GC):
                    pe.wait_ge(lo_ready, 8 * g + s + 1)
                    if s < GC:
                        pe.wait_ge(yin_ready, GC * g + s + 1)
                    else:
                        pe.wait_ge(z_ready, GC * g + s - GC + 1)
                        pe.wait_ge(ada_added, ADA_PER_G * (g + 1))
                    chunk_mm(ps[s], w_hl[:, s % 2, :, :], xT_hl, x_ready=x_lo if s == 0 else None)
                for d in range(GC):
                    for c in range(GC):
                        if d == 0:
                            pe.wait_ge(grp_lo, GC * g + c + 1)
                        f = slice(d * P, (d + 1) * P)
                        last = split_mm(ps[d][:, :], (wgrp_hi[:, c, f], wgrp_lo[:, c, f]),
                                        (pooled_hi[:, c, :], pooled_lo[:, c, :]), c == 0, c == GC - 1)
                    last.then_inc(grp_mm, 1)
                pe.wait_ge(acc_ready[0], 4 * g + 4)
                pe.wait_ge(acc_ready[1], 2 * g + 2)
                for i in range(ADA_PER_G):
                    pe.wait_ge(z_ready, GC * (g + 1) + i % GC + 1)
                    mm(ada_sum(i), lhsT=ones[:, :], rhs=adaacc[:, i, :], start=True, stop=True).then_inc(acc_mm, 1)


            def wout_mm(c, t, first, final):
                bank = ps[4 * (c // 8) + t]
                w = hl_of(NIN + c)
                for i in range(2):
                    k, f = 2 * (c % 8) + i, slice(i * T, (i + 1) * T)
                    tok = slice(t * P, (t + 1) * P)
                    last = split_mm(bank[:, :], (yin_hi[:, k, tok], yin_lo[:, k, tok]), (w[:, 0, f], w[:, 1, f]),
                                    first and i == 0, final and i == 1)
                return last

            for c in range(NWO - NRES):
                pe.wait_ge(lo_ready, NIN + c + 1)
                pe.wait_ge(yin_lo_ready, min(2 * (c % 8) + 2, NKP))
                if c == 8:
                    pe.wait_ge(ada_added, ADA_PER_G + NADA)
                for t in range(NT):
                    if c == 0:
                        pe.wait_ge(yin_ready, GC + NKP - NT + t + 1)
                    last = wout_mm(c, t, c % 8 == 0, c == 7)
                last.then_inc(w_mm, 1)
            for t in range(NT):
                for c in range(NWO - NRES, NWO):
                    if t == 0:
                        pe.wait_ge(lo_ready, NIN + c + 1)
                    last = wout_mm(c, t, False, c == NWO - 1)
                last.then_inc(yout_mm, 2)
            def transpose_h1(t):
                pe.wait_ge(h1_ready, t + 1)
                for k in range(KD):
                    bank = ps[t] if k < 4 else ps[4 + t]
                    last = nc.tensor.transpose(bank[:, (k % 4) * P:(k % 4 + 1) * P],
                                               h1tmp[:, t % 2, k * P:(k + 1) * P], ident[:, :])
                last.then_inc(h1_tr, 1)

            for t in range(NT - 1):
                transpose_h1(t)
            first = NIN + NWO
            pe.wait_ge(h1_lo, 4)
            for s in (XR, GR):
                pe.wait_ge(lo_ready, first + s + 1)
                chunk_mm(ps[s], hl_of(first + s), h1T_hl, slice(0, T // 2))
            transpose_h1(NT - 1)

            def head_means(n):
                pe.wait_ge(sq_ready, n + 1)
                if n:
                    pe.wait_ge(rn_ready, n)
                mm(ps[7][:, :], lhsT=headmean[:, :], rhs=(sqb if n % 2 == 0 else sqa)[:, 0:T],
                   start=True, stop=True).then_inc(norm_mm, 1)

            pe.wait_ge(h1_lo, 2 * NT)
            read_by = {XR: xr_copied, GR: gg_ready, GCT: gc_copied, XA: v_ready, GB: ya_ready}
            for j in range(NJ):
                for s in range(5):
                    n = NIN + NWO + 5 * j + s
                    pe.wait_ge(lo_ready, n + 1)
                    if j:
                        pe.wait_ge(read_by[s], j)
                    chunk_mm(ps[s], hl_of(n), h1T_hl, slice(T // 2 if n < first + 2 else 0, T))
                    if j and s == XR:
                        head_means(2 * j - 2)
                    if j and s == GR:
                        head_means(2 * j - 1)
                    if s == GR:
                        pe.wait_ge(bd_in, 64)
                        pe.wait_ge(cx_ready, j + 1)
                        if j:
                            pe.wait_ge(sig_ready, 2 * j)
                        mm(ps[5][:, :], lhsT=bdr[:, j, :], rhs=cx[:, 0:T], start=True, stop=True).then_inc(gates_mm, 1)
                        mm(ps[6][:, :], lhsT=bdi[:, j, :], rhs=cx[:, 0:T], start=True, stop=True).then_inc(gates_mm, 1)

            def wout2_mm(t, half, early):
                for n, k in enumerate(k for k in range(KD) if (k % NJ < NJ - 1) == early):
                    last = mm(ps[2 * t + half][:, :], lhsT=yT[:, k, t * P:(t + 1) * P],
                              rhs=wout2[:, k, half * T:(half + 1) * T], start=early and n == 0,
                              stop=not early and n == 1)
                if not early:
                    last.then_inc(y2_mm, 1)

            pe.wait_ge(yT_ready, 2 * NJ - 2)
            pe.wait_ge(wout2_in, 16)
            wout2_mm(0, 0, True)
            head_means(2 * NJ - 2)
            head_means(2 * NJ - 1)
            pe.wait_ge(gc_copied, NJ)
            pe.wait_ge(v_ready, NJ)
            wout2_mm(0, 1, True)
            wout2_mm(1, 0, True)
            pe.wait_ge(yT_ready, 2 * NJ)
            wout2_mm(0, 0, False)
            wout2_mm(0, 1, False)
            wout2_mm(1, 1, True)
            wout2_mm(1, 0, False)
            wout2_mm(1, 1, False)

            def transpose_h2(src, bank):
                for k in range(KD):
                    last = nc.tensor.transpose(ps[bank + k // 4][:, (k % 4) * P:(k % 4 + 1) * P],
                                               src[:, k * P:(k + 1) * P], ident[:, :])
                last.then_inc(h2_tr, 1)

            def query(h, bank):
                for k in range(KD):
                    last = mm(ps[bank][:, 0:P], lhsT=wq[:, k, (h % HEADS) * P:(h % HEADS + 1) * P],
                              rhs=h2T[:, k, :], start=(k == 0), stop=(k == KD - 1))
                last.then_inc(q_mm, 1)

            def score(h, bank):
                for c in range(2):
                    r = slice(DKH * c, DKH * c + DKH)
                    last = mm(ps[bank + c][:, 0:NKEYS], lhsT=qT[r, h % 2, :], rhs=keys[r, h % HEADS, :],
                              start=True, stop=True)
                last.then_inc(score_mm, 1)

            pe.wait_ge(h2_ready, 1)
            transpose_h2(h2[:, 0, :], 0)
            pe.wait_ge(wq_in, 16)
            pe.wait_ge(keys_in, 16)
            pe.wait_ge(h2T_ready, 2)
            query(0, 0)
            query(1, 1)
            pe.wait_ge(q_copied, 1)
            score(0, 6)
            pe.sem_inc(slot_free, EARLY)
            wout2_mm(2, 0, True)
            pe.wait_ge(q_copied, 2)
            pe.wait_ge(y2_read, 2)
            score(1, 2)
            wout2_mm(2, 0, False)
            wout2_mm(2, 1, True)
            wout2_mm(2, 1, False)
            pe.wait_ge(score_ready, 2)
            for half in range(2):
                for early in (True, False):
                    wout2_mm(3, half, early)
            pe.wait_ge(y2_mm, 2 * NT)
            pe.sem_inc(slot_free, RING - EARLY)
            pe.wait_ge(y2_read, NT)

            pe.sem_inc(tile_read, 2)
            pe.wait_ge(vconsts, 2)
            with pe.Fori(0, NT, 1) as t:
                pe.wait_ge(tile_read, 2 * t + 2)
                for e in range(HEADS):
                    h = e + 2
                    for n in range(TOPK):
                        pe.wait_ge(diag_ready, t * (HEADS * TOPK) + TOPK * e + n + 1)
                        for half in range(2):
                            last = mm(ps[half][:, :], lhsT=diag[:, n % RING, :],
                                      rhs=ring[:, n % RING, DM + half * T:DM + (half + 1) * T],
                                      start=(e == 0 and n == 0), stop=(e == HEADS - 1 and n == TOPK - 1))
                            if e == HEADS - 1 and n == TOPK - 1 and half == 0:
                                last.then_inc(tile_mm, 1)
                        last.then_inc(slot_free, 1)
                        if n == 1:
                            if h == HEADS:
                                pe.wait_ge(h2T_ready, 2 * t + 4)
                            query(h, 2 + h % 2)
                        if n == 5:
                            pe.wait_ge(q_copied, HEADS * t + h + 1)
                            pe.wait_ge(score_ready, 2 * HEADS * t + 2 * (h - 1))
                            score(h, 4 + 2 * (h % 2))
                        if n == 7 and h == HEADS - 1:
                            pe.wait_ge(h2n_ready, t + 1)
                            transpose_h2(h2next, 2)

        @block.scalar
        def _(act):
            def hi_part(n):
                act.wait_ge(raw_arr[n % RAW], 16 * (n // RAW + 1))
                if NIN + NWO - NRES <= n < NIN + NWO:
                    act.wait_ge(ada_added, ADA_PER_G + NADA)
                elif n >= 2:
                    act.wait_ge(w_mm, n - 1 - (NRES if n >= NIN + NWO else 0))
                nc.scalar.copy(hl_of(n)[:, 0, :], raw[:, n % RAW, :]).then_inc(hi_ready, 1)

            hi_part(0)
            for k in range(KD):
                act.wait_ge(xT_in[k // 2], 16)
                nc.scalar.copy(xT_hl[:, k, 0, :], xT_s[:, k, :]).then_inc(x_hi, 1)
            hi_part(1)
            act.wait_ge(par_in, 16)
            nc.scalar.activation(cact[:, :], pars[:, C_C:C_C + KD], ACT.Silu).then_inc(cact_ready, 1)
            act.wait_ge(lam_one, 1)
            nc.scalar.activation(lscr[:, 0, :], lscr[:, 0, :], ACT.Exp, scale=-1.0).then_inc(lam_exp, 1)
            act.wait_ge(lam_one, 2)
            nc.scalar.activation(lscr[:, 0, :], lscr[:, 0, :], ACT.Ln).then_inc(lam_ln, 1)
            act.wait_ge(vconsts, 1)

            for g in range(NG):
                for s in range(GC):
                    act.wait_ge(w_mm, 8 * g + s + 1)
                    if g:
                        act.wait_ge(m_ready, GC * (g - 1) + s + 1)
                    nc.scalar.copy(upad[:, s, PAD:], ps[s][:, :]).then_inc(u_ready, 1)
                    hi_part(8 * g + s + 2)
                    if g == 0 and s == GC - 1:
                        for n in range(6):
                            act.dma_start(ada[:, n, :], row_on_all(b_ada[n * DM:(n + 1) * DM])).then_inc(bada_in, 16)
                        act.dma_start(ntmp, row_on_all(norm1)).then_inc(ntmp_in, 16)
                for s in range(GC):
                    act.wait_ge(w_mm, 8 * g + GC + s + 1)
                    if g:
                        act.wait_ge(yin_ready, GC * g + s + 1)
                    nc.scalar.activation(zs[:, s, :], ps[GC + s][:, :], ACT.Silu).then_inc(z_ready, 1)
                    def grp_hi_parts(*chunks):
                        for c in chunks:
                            act.wait_ge(grp_arr, 16 * g + 16)
                            nc.scalar.copy(wgrp_hi[:, c, :], wgrp[:, c, :]).then_inc(grp_hi, 1)
                            act.wait_ge(m_ready, GC * g + c + 1)
                            nc.scalar.copy(pooled_hi[:, c, :], pooled[:, c, :]).then_inc(grp_hi, 1)

                    if s == 2:
                        grp_hi_parts(2, 3)
                    hi_part(8 * g + GC + s + 2)
                    if s < 2:
                        grp_hi_parts(s)
            for c in range(NKP):
                act.wait_ge(yin_ready, GC + c + 1)
                nc.scalar.copy(yin_hi[:, c, :], yin[:, c, :]).then_inc(yin_hi_ready, 1)
            for n in range(NIN + 2, NIN + NWO + 2):
                hi_part(n)

            def root_of_squares(row, junk, nth):
                act.wait_ge(row_ready, nth)
                nc.scalar.activation(junk, row, ACT.Square, accum_out=stats[:, 14:15])
                act.drain()
                nc.scalar.activation(stats[:, 14:15], stats[:, 14:15], ACT.Sqrt, scale=1.0 / DM,
                                     bias=stats[:, 15:16]).then_inc(root_ready, 1)

            for t in range(NT + 1):
                if t < NT:
                    act.wait_ge(var_ready, t + 1)
                    nc.scalar.activation(stats[:, 13:14], stats[:, 13:14], ACT.Sqrt,
                                         bias=stats[:, 16:17]).then_inc(root_ready, 1)
                    root_of_squares(xres[:, t, :], junk1, t + 1)
                if t:
                    act.wait_ge(h1_tr, t)
                    for b in range(2):
                        k, tok = slice(4 * b, 4 * b + 4), slice((t - 1) * P, t * P)
                        for dst in (h1T_hl[:, k, 0, tok], h1T[:, k, tok]):
                            nc.scalar.copy(dst, ps[4 * b + t - 1][:, :].rearrange("p (k f) -> p k f", k=4)).then_inc(h1_hi, 1)

            act.wait_ge(lrate_ready, 1)
            act.wait_ge(pads2, 1)

            def head_root(n):
                act.wait_ge(norm_mm, n + 1)
                if n:
                    act.wait_ge(yT_ready, n)
                nc.scalar.activation(rn[:, 0:T], ps[7][:, :], ACT.Sqrt, bias=stats[:, 15:16]).then_inc(rn_ready, 1)

            def next_hi(i):
                if i + 2 < 5 * NJ:
                    hi_part(NIN + NWO + i + 2)

            for j in range(NJ):
                act.wait_ge(w_mm, MM2 + 5 * j + XR + 1)
                nc.scalar.copy(xrp[:, 3:3 + T], ps[XR][:, :]).then_inc(xr_copied, 1)
                next_hi(5 * j + XR)
                if j:
                    head_root(2 * j - 2)
                act.wait_ge(w_mm, MM2 + 5 * j + GR + 1)
                next_hi(5 * j + GR)
                if j:
                    act.wait_ge(yT_ready, 2 * j - 1)
                nc.scalar.activation(gg[:, 0:T], ps[GR][:, :], ACT.Gelu).then_inc(gg_ready, 1)
                if j:
                    head_root(2 * j - 1)
                for n, (dst, bias) in enumerate(((rt, C_BR), (iu, C_BI))):
                    act.wait_ge(gates_mm, 2 * j + n + 1)
                    nc.scalar.activation(dst[:, 0:T], ps[5 + n][:, :], ACT.Sigmoid,
                                         bias=pars[:, bias + j:bias + j + 1]).then_inc(sig_ready, 1)
                act.drain()
                nc.scalar.activation(rt[:, 0:T], rt[:, 0:T], ACT.Tanh,
                                     scale=lrate[:, j:j + 1]).then_inc(tanh_ready, 1)
                act.wait_ge(w_mm, MM2 + 5 * j + GCT + 1)
                nc.scalar.copy(gcs[:, 0:T], ps[GCT][:, :]).then_inc(gc_copied, 1)
                next_hi(5 * j + GCT)
                next_hi(5 * j + XA)
                act.wait_ge(om_ready, j + 1)
                nc.scalar.activation(om[:, 0:T], om[:, 0:T], ACT.Sqrt).then_inc(om_root, 1)
                next_hi(5 * j + GB)
                act.wait_ge(yb_ready, j + 1)
                if j:
                    act.wait_ge(norm_mm, 2 * j - 1)
                nc.scalar.activation(sqb[:, 0:T], gg[:, 0:T], ACT.Square).then_inc(sq_ready, 1)
                act.wait_ge(ya_ready, j + 1)
                if j:
                    act.wait_ge(norm_mm, 2 * j)
                nc.scalar.activation(sqa[:, 0:T], ya[:, 0:T], ACT.Square).then_inc(sq_ready, 1)

            head_root(2 * NJ - 2)
            head_root(2 * NJ - 1)
            def copy_h2T(nth, bank):
                act.wait_ge(h2_tr, nth)
                for b in range(2):
                    nc.scalar.copy(h2T[:, 4 * b:4 * b + 4, :],
                                   ps[bank + b][:, :].rearrange("p (k f) -> p k f", k=4)).then_inc(h2T_ready, 1)

            def copy_q(h, bank, nth):
                act.wait_ge(q_mm, nth)
                nc.scalar.copy(qT[:, h % 2, :], ps[bank][:, 0:P]).then_inc(q_copied, 1)

            def copy_score(bank, nth):
                act.wait_ge(score_mm, nth)
                for c in range(2):
                    nc.scalar.copy(cur[:, c, :], ps[bank + c][:, 0:NKEYS]).then_inc(score_ready, 1)

            root_of_squares(xres[:, 0, :], junk2, NT + 1)
            copy_h2T(1, 0)
            root_of_squares(xres[:, 1, :], junk2, NT + 2)
            copy_q(0, 0, 1)
            copy_score(6, 1)
            copy_q(1, 1, 2)
            act.wait_ge(best_ready, 1)
            nc.scalar.activation(best[:, :], best[:, :], ACT.Exp, accum_out=esum[:, :]).then_inc(exp_ready, 1)
            act.wait_ge(idx_ready, 1)
            copy_score(2, 2)
            root_of_squares(xres[:, 2, :], junk2, NT + 3)
            root_of_squares(xres[:, 3, :], junk2, NT + 4)

            act.wait_ge(vconsts, 2)
            with act.Fori(0, NT, 1) as t:
                for e in range(HEADS):
                    step, h = t * HEADS + e, e + 2
                    for b in range(TOPK // BATCH):
                        act.wait_ge(dots_done, step * TOPK + BATCH * (b + 1))
                        nc.scalar.activation(acts[:, e % 2, BATCH * b:BATCH * (b + 1)],
                                             dots[:, e % 2, BATCH * b:BATCH * (b + 1)], ACT.Gelu).then_inc(gelu_done, 1)
                        if b == 1:
                            copy_q(h, 2 + h % 2, HEADS * t + h + 1)
                        if b == 2 and h == HEADS - 2:
                            act.wait_ge(h2_tr, t + 1)
                            nc.scalar.copy(h2next, h2[:, t + 1, :]).then_inc(h2n_ready, 1)
                        if b == 3:
                            act.wait_ge(best_ready, step + 2)
                            nc.scalar.activation(best[:, :], best[:, :], ACT.Exp,
                                                 accum_out=esum[:, :]).then_inc(exp_ready, 1)
                            act.wait_ge(idx_ready, step + 2)
                            copy_score(4 + 2 * (h % 2), HEADS * t + h + 1)
                        if b == 5 and h == HEADS - 1:
                            copy_h2T(t + 2, 2)
                root_of_squares(outb, junk2, 2 * NT + 1 + t)

        @block.vector
        def _(dve):
            tt, ts, stt = nc.vector.tensor_tensor, nc.vector.tensor_scalar, nc.vector.scalar_tensor_tensor

            for b in (upad[:, :, 0:PAD], wa[:, 0:PAD], wb[:, 0:PAD]):
                nc.vector.memset(b, 0.0)
            nc.vector.memset(stats[:, 15:16], EPS)
            nc.vector.memset(stats[:, 16:17], LN_EPS)
            nc.vector.memset(headmean[:, :], 0.0)
            dve.drain()
            for e in range(2):
                r = slice(64 * e, 64 * e + 64)
                nc.vector.memset(headmean[r, r], 1.0 / 64)
            dve.drain()
            dve.sem_inc(vconsts, 1)
            for k in range(KD):
                dve.wait_ge(x_hi, k + 1)
                tt(xT_hl[:, k, 1, :], xT_s[:, k, :], xT_hl[:, k, 0, :].bitcast(f32), ALU.subtract).then_inc(x_lo, 1)
            dve.wait_ge(consts, 5)
            nc.vector.reciprocal(invcnt[:, :], invcnt[:, :])
            dve.wait_ge(cact_ready, 1)
            dve.wait_ge(par_in, 16)
            lam = pars[:, C_LAM:C_LAM + NJ]
            ts(lscr[:, 1, :], lam, -1.0, None, ALU.mult)
            dve.drain()
            tt(lscr[:, 0, :], lam, lscr[:, 1, :], ALU.max).then_inc(lam_one, 1)
            dve.drain()
            ts(lscr[:, 1, :], lscr[:, 1, :], 0.0, None, ALU.max)
            dve.wait_ge(lam_exp, 1)
            ts(lscr[:, 0, :], lscr[:, 0, :], 1.0, None, ALU.add).then_inc(lam_one, 1)
            dve.wait_ge(lam_ln, 1)
            tt(lrate[:, :], lscr[:, 0, :], lscr[:, 1, :], ALU.add)
            dve.drain()
            ts(lrate[:, :], lrate[:, :], -4.0, None, ALU.mult).then_inc(lrate_ready, 1)

            def ada_block(b):
                dve.wait_ge(ada_arr[b % ADA_RING], 16 * (b // ADA_RING + 1))
                if b >= ADA_PER_G:
                    dve.wait_ge(acc_mm, b - ADA_PER_G + 1)
                dst = adaacc[:, b % ADA_PER_G, :]
                for k in range(KD):
                    w = adaring[:, b % ADA_RING, k, :]
                    if k == 0:
                        last = ts(dst, w, cact[:, 0:1], None, ALU.mult)
                    else:
                        dve.drain()
                        last = stt(dst, w, cact[:, k:k + 1], dst, ALU.mult, ALU.add)
                last.then_inc(acc_ready[0], 1)
                dve.wait_ge(acc_ready[0], 4 * (b // ADA_PER_G) + (0, 2, 4, 5).index(b % ADA_PER_G) + 1)
                dve.sem_inc(ada_used[b % ADA_RING], 1)

            def ada_add(b):
                dve.wait_ge(acc_mm, ADA_PER_G * (b // ADA_PER_G + 1))
                q, c = b // 4, (b % 4) * ADA_W
                dst = ada[:, q, c:c + ADA_W]
                dve.wait_ge(bada_in, 96)
                last = tt(dst, ada_sum(b % ADA_PER_G), dst, ALU.add)
                if q in (1, 4):
                    dve.wait_ge(ntmp_in, 16 if q == 1 else 32)
                    dve.drain()
                    last = stt(dst, dst, 1.0, ntmp[:, c:c + ADA_W], ALU.add, ALU.mult)
                last.then_inc(ada_added, 1)

            def window(g, s):
                w = WINDOWS[g]
                dve.wait_ge(u_ready, GC * g + s + 1)
                dve.drain()
                src, shift = upad[:, s, :], 1
                for i in range(g + 1):
                    dst = wa if i % 2 == 0 else wb
                    tt(dst[:, PAD:], src[:, PAD:], src[:, PAD - shift:PAD + T - shift], ALU.add)
                    dve.drain()
                    src, shift = dst, 2 * shift
                other = wb if g % 2 == 0 else wa
                if g and s == 0:
                    dve.wait_ge(grp_mm, GC * g)
                stt(pooled[:, s, :], src[:, PAD:], 1.0 / w, upad[:, s, PAD:], ALU.mult, ALU.subtract)
                tt(other[:, PAD:PAD + w - 1], src[:, PAD:PAD + w - 1], invcnt[:, 0:w - 1], ALU.mult)
                dve.drain()
                tt(pooled[:, s, 0:w - 1], other[:, PAD:PAD + w - 1], upad[:, s, PAD:PAD + w - 1],
                   ALU.subtract).then_inc(m_ready, 1)

            def yin_lo_part(c):
                dve.wait_ge(yin_hi_ready, c + 1)
                tt(yin_lo[:, c, :], yin[:, c, :], yin_hi[:, c, :].bitcast(f32), ALU.subtract).then_inc(yin_lo_ready, 1)

            for g in range(NG):
                for s in range(GC):
                    if s % 2 == 0:
                        ada_block(ADA_PER_G * g + s)
                    window(g, s)
                ada_block(ADA_PER_G * g + GC)
                for c in range(GC):
                    for n, (dst, src, hi) in enumerate(((wgrp_lo, wgrp, wgrp_hi), (pooled_lo, pooled, pooled_hi))):
                        dve.wait_ge(grp_hi, 2 * GC * g + 2 * c + n + 1)
                        last = tt(dst[:, c, :], src[:, c, :], hi[:, c, :].bitcast(f32), ALU.subtract)
                    last.then_inc(grp_lo, 1)
                ada_block(ADA_PER_G * g + 5)
                if g == NG - 1:
                    for c in range(NKP - GC):
                        yin_lo_part(c)
                for d in range(GC):
                    dve.wait_ge(grp_mm, GC * g + d + 1)
                    dve.wait_ge(z_ready, GC * (g + 1) + d + 1)
                    c = GC * g + d
                    stt(yin[:, c, :], ps[d][:, :], pars[:, C_SCALE + c:C_SCALE + c + 1], zs[:, d, :],
                        ALU.mult, ALU.mult).then_inc(yin_ready, 1)
                if g == NG - 1:
                    for c in range(NKP - GC, NKP):
                        yin_lo_part(c)
                for i in range(ADA_PER_G):
                    ada_add(ADA_PER_G * g + i)

            def inverse_root(col, nth):
                dve.wait_ge(root_ready, nth)
                nc.vector.reciprocal(stats[:, col:col + 1], stats[:, col:col + 1])
                dve.drain()

            dve.wait_ge(x_in, 16 * NT)
            dve.wait_ge(ln_in, 32)
            for t in range(NT):
                dve.wait_ge(yout_mm, 2 * (t + 1))
                row, h1 = xres[:, t, :], h1tmp[:, t % 2, :]
                for half in range(2):
                    c = slice(half * T, (half + 1) * T)
                    stt(row[:, c], row[:, c], ALPHA, ps[4 * half + t][:, :], ALU.mult, ALU.add)
                    dve.drain()
                    nc.vector.bn_stats(stats[:, 6 * half:6 * half + 6], row[:, c])
                dve.drain()
                nc.vector.bn_aggr(stats[:, 12:14],
                                  stats[:, 0:12].rearrange("p (a b) -> p a b", a=2)).then_inc(var_ready, 1)
                dve.drain()
                stt(row, row, stats[:, 12:13], lnw[:, 0, :], ALU.subtract, ALU.mult)
                inverse_root(13, 2 * t + 1)
                stt(row, row, stats[:, 13:14], lnw[:, 1, :], ALU.mult, ALU.add).then_inc(row_ready, 1)
                dve.drain()
                if t >= 2:
                    dve.wait_ge(h1_tr, t - 1)
                tt(h1, row, ada[:, 1, :], ALU.mult)
                inverse_root(14, 2 * t + 2)
                stt(h1, h1, stats[:, 14:15], ada[:, 0, :], ALU.mult, ALU.add).then_inc(h1_ready, 1)

            dve.wait_ge(h1_lo, 2 * NT)
            nc.vector.memset(xrp[:, 0:3], 0.0)
            nc.vector.memset(vp[:, 0:2], 0.0)
            dve.drain()
            dve.sem_inc(pads2, 1)

            def par(col, j):
                return pars[:, col + j:col + j + 1]

            def head_norm(n):
                j = n // 2
                y, gn, k = (gg, C_GNB, NJ + j) if n % 2 == 0 else (ya, C_GNA, j)
                dve.wait_ge(rn_ready, n + 1)
                nc.vector.reciprocal(rn[:, 0:T], rn[:, 0:T])
                dve.drain()
                stt(yT[:, k, :], y[:, 0:T], par(gn, j), rn[:, 0:T], ALU.mult, ALU.mult).then_inc(yT_ready, 1)

            for j in range(NJ):
                dve.wait_ge(xr_copied, j + 1)
                w = C_CONVB + 4 * j
                c = cx[:, 0:T]
                ts(c, xrp[:, 0:T], pars[:, w:w + 1], par(C_CBB, j), ALU.mult, ALU.add)
                for k in range(1, 4):
                    dve.drain()
                    last = stt(c, xrp[:, k:k + T], pars[:, w + k:w + k + 1], c, ALU.mult, ALU.add)
                last.then_inc(cx_ready, 1)
                if j:
                    head_norm(2 * j - 2)
                    head_norm(2 * j - 1)
                dve.wait_ge(tanh_ready, j + 1)
                th, d, a, o = rt[:, 0:T], den[:, 0:T], aa[:, 0:T], om[:, 0:T]
                u, h, y = iu[:, 0:T], hh[:, 0:T], gg[:, 0:T]
                ts(d, th, -1.0, 1.0, ALU.mult, ALU.add)
                tt(u, u, c, ALU.mult)
                dve.drain()
                nc.vector.reciprocal(d, d)
                dve.drain()
                stt(a, th, 1.0, d, ALU.add, ALU.mult)
                stt(o, th, -2.0, d, ALU.mult, ALU.mult)
                dve.drain()
                stt(o, a, 1.0, o, ALU.add, ALU.mult)
                dve.drain()
                ts(o, o, 0.0, None, ALU.max).then_inc(om_ready, 1)
                dve.wait_ge(w_mm, MM2 + 5 * j + XA + 1)
                dve.wait_ge(gc_copied, j + 1)
                tt(vp[:, 2:2 + T], gcs[:, 0:T], ps[XA][:, :], ALU.mult).then_inc(v_ready, 1)
                dve.drain()
                w = C_CONVA + 3 * j
                ca = ya[:, 0:T]
                ts(ca, vp[:, 0:T], pars[:, w:w + 1], None, ALU.mult)
                for k in range(1, 3):
                    dve.drain()
                    stt(ca, vp[:, k:k + T], pars[:, w + k:w + k + 1], ca, ALU.mult, ALU.add)
                dve.wait_ge(om_root, j + 1)
                tt(u, u, o, ALU.mult)
                dve.drain()
                nc.vector.tensor_tensor_scan(h, a, u, 0.0, ALU.mult, ALU.add)
                dve.drain()
                dve.wait_ge(gg_ready, j + 1)
                tt(y, y, h, ALU.mult).then_inc(yb_ready, 1)
                dve.wait_ge(w_mm, MM2 + 5 * j + GB + 1)
                tt(ca, ca, ps[GB][:, :], ALU.mult).then_inc(ya_ready, 1)
            head_norm(2 * NJ - 2)
            head_norm(2 * NJ - 1)

            def make_h2(t):
                dve.wait_ge(y2_mm, 2 * t + 2)
                row, hrow = xres[:, t, :], h2[:, t, :]
                dve.drain()
                for half in range(2):
                    c = slice(half * T, (half + 1) * T)
                    last = tt(xtmp[:, c], ps[2 * t + half][:, :], ada[:, 2, c], ALU.mult)
                last.then_inc(y2_read, 1)
                dve.drain()
                tt(row, row, xtmp, ALU.add).then_inc(row_ready, 1)
                dve.drain()
                tt(hrow, row, ada[:, 4, :], ALU.mult)
                inverse_root(14, 2 * NT + t + 1)
                stt(hrow, hrow, stats[:, 14:15], ada[:, 3, :], ALU.mult, ALU.add).then_inc(h2_ready, 1)

            make_h2(0)
            make_h2(1)

            cf = cand.rearrange("p a b -> p (a b)")

            def choose(part, to):
                dve.drain()
                if part < 2:
                    c = part
                    nc.vector.max(topv[:, c, 0:8], cur[:, c, :])
                    dve.drain()
                    nc.vector.max_index(topi[:, c, 0:8], topv[:, c, 0:8], cur[:, c, :])
                    nc.vector.match_replace(rest[:, 0:NKEYS], topv[:, c, 0:8], cur[:, c, :], LOWEST)
                    dve.drain()
                    nc.vector.max(topv[:, c, 8:16], rest[:, 0:NKEYS])
                    dve.drain()
                    nc.vector.max_index(topi[:, c, 8:16], topv[:, c, 8:16], rest[:, 0:NKEYS])
                    dve.drain()
                    ts(topf[:, c, :], topi[:, c, :], float(NKEYS) if c == 0 else 1.0, None, ALU.mult)
                if part == 2:
                    tt(cand, topv[:, 0, :].unsqueeze(2).to_broadcast([P, TOPK, TOPK]),
                       topv[:, 1:2, :].to_broadcast([P, TOPK, TOPK]), ALU.add)
                    dve.drain()
                    nc.vector.max(best[:, 0:8], cf)
                    dve.drain()
                    nc.vector.max_index(bpos[:, 0:8], best[:, 0:8], cf)
                    nc.vector.match_replace(rest, best[:, 0:8], cf, LOWEST)
                if part == 3:
                    nc.vector.max(best[:, 8:16], rest)
                    dve.drain()
                    nc.vector.max_index(bpos[:, 8:16], best[:, 8:16], rest)
                    nc.vector.tensor_copy(top1[:, :], best[:, 0:1])
                    dve.drain()
                    ts(ab[:, :, 0], bpos[:, :], 4, None, ALU.logical_shift_right)
                    ts(ab[:, :, 1], bpos[:, :], TOPK - 1, None, ALU.bitwise_and)
                    ts(best[:, :], best[:, :], top1[:, 0:1], None, ALU.subtract).then_inc(best_ready, 1)
                    dve.drain()
                    nc.vector.tensor_copy(abf[:, :, :], ab[:, :, :])
                if part == 4:
                    tt(hot, abf[:, :, :].unsqueeze(3).to_broadcast([P, TOPK, 2, TOPK]),
                       iota16[:, :].unsqueeze(1).unsqueeze(1).to_broadcast([P, TOPK, 2, TOPK]), ALU.is_equal)
                    dve.drain()
                    tt(hot, hot, topf[:, :, :].unsqueeze(1).to_broadcast([P, TOPK, 2, TOPK]), ALU.mult)
                    dve.drain()
                    nc.vector.tensor_reduce(idxf, hot.rearrange("p k c a -> p k (c a)"), AX.X, ALU.add)
                    dve.drain()
                    nc.vector.tensor_copy(idx[:, to, :], idxf).then_inc(idx_ready, 1)
                if part == 5:
                    nc.vector.reciprocal(esum[:, :], esum[:, :])
                    dve.drain()
                    ts(gate[:, to, :], best[:, :], esum[:, 0:1], None, ALU.mult)
                    dve.drain()

            dve.wait_ge(score_ready, 2)
            for part in range(5):
                choose(part, 0)
            dve.wait_ge(exp_ready, 1)
            choose(5, 0)
            make_h2(2)
            dve.wait_ge(score_ready, 4)
            choose(0, 1)
            choose(1, 1)
            make_h2(3)
            nc.vector.memset(h2[:, NT, :], 0.0)
            dve.drain()
            dve.sem_inc(vconsts, 1)
            dve.sem_inc(outb_free, 1)

            nc.vector.tensor_copy(h2cur, h2[:, 0, :])
            dve.drain()
            beside = {0: 2, 1: 3, 2: 4, 4: 5, 5: 0, 6: 1}
            with dve.Fori(0, NT, 1) as t:
                with dve.Fori(0, HEADS // 2, 1) as i:
                    for e in range(2):
                        step = t * HEADS + i * 2 + e
                        for b in range(TOPK // BATCH):
                            for n in range(BATCH * b, BATCH * (b + 1)):
                                dve.wait_ge(arr[n % RING], step * (16 * TOPK // RING) + 16 * (n // RING + 1))
                                urow = ring[:, n % RING, 0:DM]
                                nc.vector.tensor_tensor_reduce(
                                    out=urow, in0=urow, in1=h2cur, scale=1.0, scalar=0.0, op0=ALU.mult,
                                    op1=ALU.add, accum_out=dots[:, e, n:n + 1]).then_inc(dots_done, 1)
                            if b in beside:
                                part = beside[b]
                                if part == 0:
                                    dve.wait_ge(score_ready, 2 * step + 6)
                                    dve.sem_inc(vec_go, 1)
                                if part == 5:
                                    dve.wait_ge(exp_ready, step + 2)
                                    dve.sem_inc(vec_go, 1)
                                choose(part, 1 - e)
                            dve.wait_ge(gelu_done, step * (TOPK // BATCH) + b + 1)
                            for n in range(BATCH * b, BATCH * (b + 1)):
                                ts(diag[:, n % RING, :], ident[:, :], acts[:, e, n:n + 1], gate[:, e, n:n + 1],
                                   ALU.mult, ALU.mult).then_inc(diag_ready, 1)
                dve.wait_ge(fing_in, 16)
                dve.wait_ge(outb_free, t + 1)
                for half in range(2):
                    if half == 0:
                        dve.wait_ge(tile_mm, t + 1)
                    else:
                        dve.wait_ge(slot_free, (t + 1) * (HEADS * TOPK) + RING)
                    c = slice(half * T, (half + 1) * T)
                    tt(outb[:, c], ps[half][:, :], ada[:, 5, c], ALU.mult).then_inc(tile_read, 1)
                    dve.drain()
                    last = tt(outb[:, c], outb[:, c], xres[:, t, c], ALU.add)
                last.then_inc(row_ready, 1)
                nc.vector.tensor_copy(h2cur, h2[:, t + 1, :])
                inverse_root(14, 3 * NT + 1 + t)
                for half in range(2):
                    c = slice(half * T, (half + 1) * T)
                    stt(outb[:, c], outb[:, c], stats[:, 14:15], fing[:, c], ALU.mult, ALU.mult).then_inc(out_ready, 1)


_OUT = (1, T, DM)


def kernel(**inputs):
    import numpy as np
    import concourse.bacc as bacc
    from concourse.bass_utils import run_bass_kernel_spmd

    a = {k: np.asarray(v) for k, v in inputs.items()}

    def channels(v):
        v = v.reshape(-1, v.shape[-1] // P, P)
        return v.transpose(2, 1, 0).reshape(P, -1)

    def k_major(w):
        return w.reshape(-1, P, w.shape[-1]).transpose(1, 0, 2).reshape(P, -1)

    w_in = a["pool_w_in"][0].reshape(KD, P, 2, NG, GC, P)
    w_in = w_in.transpose(3, 2, 4, 1, 0, 5).reshape(NG, 2 * GC, P, DM)
    w_in2 = a["w_in_2"][0].reshape(KD, P, 5, NJ, P)
    w_in2 = w_in2[:, :, [3, 4, 1, 2, 0]].transpose(3, 2, 1, 0, 4).reshape(NJ, 5, P, DM)
    w_ada = a["w_ada_2"][0].reshape(KD, P, NADA, ADA_W).transpose(2, 1, 0, 3).reshape(NADA, P, KD * ADA_W)
    arrays = {
        "x": a["x"][0],
        "xT": a["x"][0].T,
        "par": np.concatenate([
            channels(a["c_2"]), channels(a["pool_scale"]), channels(a["conv_a_w_2"][0]),
            channels(a["conv_b_w_2"][0]), channels(a["conv_b_b_2"]), channels(a["b_r_2"].reshape(1, -1)),
            channels(a["b_i_2"].reshape(1, -1)), channels(a["lru_lambda_2"].reshape(1, -1)), channels(a["gn_a_2"]),
            channels(a["gn_b_2"])], axis=1),
        "ln_g": a["ln_g"][0], "ln_b": a["ln_b"][0],
        "w_in": w_in,
        "w_grp": a["pool_w_grp"][0].reshape(NG, GC, P, T).transpose(0, 2, 1, 3).reshape(NG, P, GC * T),
        "w_out": a["pool_w_out"][0].reshape(8, 2, P, 2, T).transpose(3, 0, 2, 1, 4).reshape(NWO, P, DM),
        "w_ada": w_ada,
        "b_ada": a["b_ada_2"][0], "norm1": a["norm1_g_2"][0],
        "w_in2": w_in2,
        "w_r": a["w_r_2"][0].reshape(NJ, 2, 64, 64).transpose(1, 2, 0, 3),
        "w_i": a["w_i_2"][0].reshape(NJ, 2, 64, 64).transpose(1, 2, 0, 3),
        "w_out2": k_major(a["w_out_2"][0]), "norm2": a["norm2_g_2"][0],
        "w_q": k_major(a["w_q_2"][0]),
        "keysT": a["sub_keys_2"][0].transpose(1, 3, 0, 2).reshape(P, HEADS * NKEYS),
        "experts": np.concatenate([a["expert_u_2"][0], a["expert_v_2"][0]], axis=1),
        "final_g": a["final_g_2"],
    }
    nc = bacc.Bacc("TRN2", target_bir_lowering=False, num_devices=1)
    feeds, args = {}, []
    for name, v in arrays.items():
        v = np.ascontiguousarray(v)
        feeds[f"in_{name}"] = v
        args.append(nc.dram_tensor(f"in_{name}", v.shape, mybir.dt.from_np(v.dtype), kind="ExternalInput").ap())
    args.append(nc.dram_tensor("out_x", (T, DM), mybir.dt.float32, kind="ExternalOutput").ap())
    mixers_and_peer(nc, *args)
    r = run_bass_kernel_spmd(nc, [feeds], core_ids=[0])
    return r.results[0]["out_x"].reshape(_OUT)
```
